# Optimizing a Trainium2 kernel written in Bass

```python
import math
import jax, jax.numpy as jnp
from jax import lax
import numpy as np

D_MODEL = 1024
BATCH = 1
SEQ = 256
DEPTH = 2

GRID_W = 64
CTX_LEN = 256
NORM_EPS = 1e-6
N_MOD = 6
HEAD_DIM = 64
N_Q_HEADS = 8
N_KV_HEADS = 2
GROUP = N_Q_HEADS // N_KV_HEADS
ATTN_W = N_Q_HEADS * HEAD_DIM
KV_W = N_KV_HEADS * HEAD_DIM
Q_BLOCK = 128
ROPE_THETA = 10000.0
HYENA_W = D_MODEL // 4
HYENA_SHORT = 3
HYENA_BANDS = 16
HYENA_EMB = 1 + 2 * HYENA_BANDS
HYENA_FFN = 64
HYENA_FAST_DECAY = 0.3
HYENA_SLOW_DECAY = 1.5
HYENA_TARGET = 1e-2
CONF_W = D_MODEL // 4
CONF_K = 31
N_BRANCH = 3
K_OFF = ATTN_W
HY_OFF = K_OFF + 2 * KV_W
CF_OFF = HY_OFF + 3 * HYENA_W
G_OFF = CF_OFF + 2 * CONF_W
IN_W = G_OFF + N_BRANCH * D_MODEL
N_EXPERTS = 16
N_GROUPS = 4
TOPK_GROUPS = 1
TOP_K = 2
EXPERT_FF = D_MODEL // 2

kernel_name = "hybrid_gated_attn_hyena_conformer_moe"

F32 = jnp.float32

def rms_norm(x, g):
    xf = x.astype(F32)
    y = xf * lax.rsqrt(jnp.mean(xf * xf, axis=-1, keepdims=True) + NORM_EPS)
    return (y * g.astype(F32)).astype(x.dtype)

def layer_norm(x, g, b):
    xf = x.astype(F32)
    mu = jnp.mean(xf, axis=-1, keepdims=True)
    var = jnp.mean(jnp.square(xf - mu), axis=-1, keepdims=True)
    y = (xf - mu) * lax.rsqrt(var + NORM_EPS) * g.astype(F32) + b.astype(F32)
    return y.astype(x.dtype)

def modulate(h, shift, scale):
    return h * (1 + scale) + shift

def depthwise_conv(x, w, b):
    k = w.shape[0]
    pad = (k - 1) // 2
    y = lax.conv_general_dilated(x, w[:, None, :].astype(x.dtype), window_strides=(1,),
                                 padding=[(pad, pad)], dimension_numbers=("NWC", "WIO", "NWC"),
                                 feature_group_count=x.shape[-1])
    return y + b.astype(x.dtype)

def heads(z, n):
    return z.reshape(z.shape[:-1] + (n, HEAD_DIM))

def axial_rope_tables(n_tokens):
    rows = n_tokens // GRID_W
    row_ids = jnp.repeat(jnp.arange(rows), GRID_W).astype(F32)
    col_ids = jnp.tile(jnp.arange(GRID_W), rows).astype(F32)
    half = HEAD_DIM // 2
    inv = ROPE_THETA ** (-jnp.arange(0, half, 2, dtype=F32) / half)
    ang_r = row_ids[:, None] * inv
    ang_c = col_ids[:, None] * inv
    ang = jnp.concatenate([ang_r, ang_r, ang_c, ang_c], axis=-1)
    return jnp.cos(ang), jnp.sin(ang)

def apply_rope(x, cos, sin):
    xf = x.astype(F32)
    x1, x2, x3, x4 = jnp.split(xf, 4, axis=-1)
    rot = jnp.concatenate([-x2, x1, -x4, x3], axis=-1)
    return (xf * cos[:, None, :] + rot * sin[:, None, :]).astype(x.dtype)

def split_kv(z_kv, k_gain):
    k = rms_norm(heads(z_kv[..., :KV_W], N_KV_HEADS), k_gain)
    v = heads(z_kv[..., KV_W:], N_KV_HEADS)
    return k, v

def latent_attention(q, k, v, k_ctx, v_ctx):
    b, s = q.shape[:2]
    keys = jnp.concatenate([k, k_ctx], axis=1)
    vals = jnp.concatenate([v, v_ctx], axis=1)
    nblk = s // Q_BLOCK
    qb = q.reshape(b, nblk, Q_BLOCK, N_KV_HEADS, GROUP, HEAD_DIM).transpose(1, 0, 2, 3, 4, 5)
    scale = 1.0 / math.sqrt(HEAD_DIM)

    def block(q_blk):
        sc = jnp.einsum("bqkgd,bskd->bkgqs", q_blk, keys, preferred_element_type=F32) * scale
        p = jax.nn.softmax(sc, axis=-1).astype(vals.dtype)
        return jnp.einsum("bkgqs,bskd->bqkgd", p, vals)

    out = lax.map(block, qb)
    return out.transpose(1, 0, 2, 3, 4, 5).reshape(b, s, ATTN_W)

def context_attention(q, k, v):
    b, n = q.shape[:2]
    qg = q.reshape(b, n, N_KV_HEADS, GROUP, HEAD_DIM)
    sc = jnp.einsum("bqkgd,bskd->bkgqs", qg, k, preferred_element_type=F32) / math.sqrt(HEAD_DIM)
    p = jax.nn.softmax(sc, axis=-1).astype(v.dtype)
    return jnp.einsum("bkgqs,bskd->bqkgd", p, v).reshape(b, n, ATTN_W)

def hyena_filter(n, lp):
    t = jnp.linspace(0.0, 1.0, n, dtype=F32)[:, None]
    w = 2.0 * math.pi * jnp.arange(n, dtype=F32)[:, None] / n
    f = jnp.linspace(1e-4, HYENA_BANDS - 1, HYENA_BANDS, dtype=F32)[None, :]
    feat = jnp.concatenate([t, jnp.cos(f * w), -jnp.sin(f * w)], axis=-1)
    freq = lp["hy_freq"].astype(F32)
    h = jnp.sin(freq * (feat @ lp["hy_w1"].astype(F32) + lp["hy_b1"].astype(F32)))
    h = jnp.sin(freq * (h @ lp["hy_w2"].astype(F32) + lp["hy_b2"].astype(F32)))
    h = h @ lp["hy_w3"].astype(F32)
    max_decay = math.log(HYENA_TARGET) / HYENA_FAST_DECAY
    min_decay = math.log(HYENA_TARGET) / HYENA_SLOW_DECAY
    deltas = jnp.tile(jnp.linspace(min_decay, max_decay, HYENA_W, dtype=F32), 2)
    h = h * jnp.exp(-t * jnp.abs(deltas))
    h = h / jnp.sum(jnp.abs(h), axis=0, keepdims=True)
    return h[:, :HYENA_W], h[:, HYENA_W:]

def bidir_fftconv(u, h_f, h_b, d_bias):
    n = u.shape[1]
    kern = jnp.concatenate([h_f, jnp.zeros((1, HYENA_W), F32), h_b[1:][::-1]], axis=0)
    uf = jnp.fft.rfft(u.astype(F32), n=2 * n, axis=1)
    kf = jnp.fft.rfft(kern, n=2 * n, axis=0)
    y = jnp.fft.irfft(uf * kf[None], n=2 * n, axis=1)[:, :n]
    return (y + u.astype(F32) * d_bias.astype(F32)).astype(u.dtype)

def hyena(z, lp):
    z = depthwise_conv(z, lp["hy_short_w"], lp["hy_short_b"])
    x0, x1, v = jnp.split(z, 3, axis=-1)
    h_f, h_b = hyena_filter(z.shape[1], lp)
    return bidir_fftconv(v * x1, h_f, h_b, lp["hy_bias"]) * x0

def conformer_conv(z, lp):
    a, g = jnp.split(z, 2, axis=-1)
    u = depthwise_conv(a * jax.nn.sigmoid(g), lp["cf_dw_w"], lp["cf_dw_b"])
    return jax.nn.silu(layer_norm(u, lp["cf_ln_g"], lp["cf_ln_b"]))

def branch_merge(z, o_attn, lp):
    o_hy = hyena(z[..., HY_OFF:CF_OFF], lp)
    o_cf = conformer_conv(z[..., CF_OFF:G_OFF], lp)
    g_a, g_h, g_c = jnp.split(jax.nn.sigmoid(z[..., G_OFF:]), N_BRANCH, axis=-1)
    merged = (g_a * (o_attn @ lp["p_attn"]) + g_h * (o_hy @ lp["p_hyena"])
              + g_c * (o_cf @ lp["p_conv"]))
    return merged @ lp["w_out"]

def moe(h, w_router, b_router, w_gate, w_up, w_down):
    shp = h.shape
    t = h.reshape(-1, D_MODEL)
    s = jax.nn.sigmoid((t @ w_router).astype(F32))
    sel = s + b_router.astype(F32)
    grp = sel.reshape(-1, N_GROUPS, N_EXPERTS // N_GROUPS)
    grp_score = jnp.sum(lax.top_k(grp, TOP_K)[0], axis=-1)
    _, gidx = lax.top_k(grp_score, TOPK_GROUPS)
    gmask = jnp.any(gidx[..., None] == jnp.arange(N_GROUPS), axis=1)
    emask = jnp.repeat(gmask, N_EXPERTS // N_GROUPS, axis=1)
    _, eidx = lax.top_k(jnp.where(emask, sel, -jnp.inf), TOP_K)
    wts = jnp.take_along_axis(s, eidx, axis=1)
    wts = wts / jnp.sum(wts, axis=-1, keepdims=True)
    combine = jnp.sum(jax.nn.one_hot(eidx, N_EXPERTS, dtype=F32) * wts[..., None], axis=1).astype(t.dtype)
    out = jnp.zeros_like(t)
    for e in range(N_EXPERTS):
        y = (jax.nn.silu(t @ w_gate[e]) * (t @ w_up[e])) @ w_down[e]
        out = out + combine[:, e:e + 1] * y
    return out.reshape(shp)

def setup_inputs(seed: int = 0) -> dict:
    key = jax.random.key(seed)
    ks = iter(jax.random.split(key, 40))

    def nrm(shape, scale):
        return jax.random.normal(next(ks), shape, F32) * scale

    L, D = DEPTH, D_MODEL
    return {
        "x": nrm((BATCH, SEQ, D), 1.0),
        "c": nrm((BATCH, D), 1.0),
        "ctx": nrm((BATCH, CTX_LEN, D), 1.0),
        "c_ctx": nrm((D,), 1.0),
        "w_mod": nrm((L, D, N_MOD * D), 0.5 * D ** -0.5),
        "b_mod": nrm((L, N_MOD * D), 0.01),
        "g_norm1": 1.0 + nrm((L, D), 0.01),
        "g_norm2": 1.0 + nrm((L, D), 0.01),
        "w_in": nrm((L, D, IN_W), D ** -0.5),
        "q_norm": 1.0 + nrm((L, HEAD_DIM), 0.01),
        "k_norm": 1.0 + nrm((L, HEAD_DIM), 0.01),
        "hy_short_w": nrm((L, HYENA_SHORT, 3 * HYENA_W), HYENA_SHORT ** -0.5),
        "hy_short_b": nrm((L, 3 * HYENA_W), 0.01),
        "hy_w1": nrm((L, HYENA_EMB, HYENA_FFN), HYENA_EMB ** -0.5),
        "hy_b1": nrm((L, HYENA_FFN), 0.01),
        "hy_w2": nrm((L, HYENA_FFN, HYENA_FFN), HYENA_FFN ** -0.5),
        "hy_b2": nrm((L, HYENA_FFN), 0.01),
        "hy_w3": nrm((L, HYENA_FFN, 2 * HYENA_W), HYENA_FFN ** -0.5),
        "hy_freq": 1.0 + nrm((L, HYENA_FFN), 0.01),
        "hy_bias": nrm((L, HYENA_W), 0.1),
        "cf_dw_w": nrm((L, CONF_K, CONF_W), CONF_K ** -0.5),
        "cf_dw_b": nrm((L, CONF_W), 0.01),
        "cf_ln_g": 1.0 + nrm((L, CONF_W), 0.01),
        "cf_ln_b": nrm((L, CONF_W), 0.01),
        "p_attn": nrm((L, ATTN_W, D), ATTN_W ** -0.5),
        "p_hyena": nrm((L, HYENA_W, D), HYENA_W ** -0.5),
        "p_conv": nrm((L, CONF_W, D), CONF_W ** -0.5),
        "w_out": nrm((L, D, D), D ** -0.5),
        "w_router": nrm((D, N_EXPERTS), D ** -0.5),
        "b_router": nrm((N_EXPERTS,), 0.01),
        "w_exp_gate": nrm((L, N_EXPERTS, D, EXPERT_FF), D ** -0.5),
        "w_exp_up": nrm((L, N_EXPERTS, D, EXPERT_FF), D ** -0.5),
        "w_exp_down": nrm((L, N_EXPERTS, EXPERT_FF, D), EXPERT_FF ** -0.5),
    }

def reference(x, c, ctx, c_ctx, w_mod, b_mod, g_norm1, g_norm2, w_in, q_norm, k_norm,
              hy_short_w, hy_short_b, hy_w1, hy_b1, hy_w2, hy_b2, hy_w3, hy_freq, hy_bias,
              cf_dw_w, cf_dw_b, cf_ln_g, cf_ln_b, p_attn, p_hyena, p_conv, w_out,
              w_router, b_router, w_exp_gate, w_exp_up, w_exp_down):
    s = x.shape[1]
    cos, sin = axial_rope_tables(s)
    xc = ctx
    for l in range(DEPTH):
        last = l == DEPTH - 1
        lp = {
            "hy_short_w": hy_short_w[l], "hy_short_b": hy_short_b[l],
            "hy_w1": hy_w1[l], "hy_b1": hy_b1[l], "hy_w2": hy_w2[l], "hy_b2": hy_b2[l],
            "hy_w3": hy_w3[l], "hy_freq": hy_freq[l], "hy_bias": hy_bias[l],
            "cf_dw_w": cf_dw_w[l], "cf_dw_b": cf_dw_b[l], "cf_ln_g": cf_ln_g[l], "cf_ln_b": cf_ln_b[l],
            "p_attn": p_attn[l], "p_hyena": p_hyena[l], "p_conv": p_conv[l], "w_out": w_out[l],
        }
        sh1, sc1, gt1, sh2, sc2, gt2 = jnp.split(
            (jax.nn.silu(c) @ w_mod[l] + b_mod[l])[:, None, :], N_MOD, axis=-1)
        csh1, csc1, cgt1, csh2, csc2, cgt2 = jnp.split(
            jax.nn.silu(c_ctx) @ w_mod[l] + b_mod[l], N_MOD, axis=-1)

        hx = modulate(rms_norm(x, g_norm1[l]), sh1, sc1)
        hc = modulate(rms_norm(xc, g_norm1[l]), csh1, csc1)
        zx = hx @ w_in[l]
        if last:
            zc_kv = hc @ w_in[l][:, K_OFF:HY_OFF]
        else:
            zc = hc @ w_in[l]
            zc_kv = zc[..., K_OFF:HY_OFF]
        kc, vc = split_kv(zc_kv, k_norm[l])
        qx = apply_rope(rms_norm(heads(zx[..., :K_OFF], N_Q_HEADS), q_norm[l]), cos, sin)
        kx, vx = split_kv(zx[..., K_OFF:HY_OFF], k_norm[l])
        kx = apply_rope(kx, cos, sin)
        o_attn_x = latent_attention(qx, kx, vx, kc, vc)
        x = x + gt1 * branch_merge(zx, o_attn_x, lp)

        hx2 = modulate(rms_norm(x, g_norm2[l]), sh2, sc2)
        if last:
            x = x + gt2 * moe(hx2, w_router, b_router, w_exp_gate[l], w_exp_up[l], w_exp_down[l])
        else:
            qc = rms_norm(heads(zc[..., :K_OFF], N_Q_HEADS), q_norm[l])
            o_attn_c = context_attention(qc, kc, vc)
            xc = xc + cgt1 * branch_merge(zc, o_attn_c, lp)
            hc2 = modulate(rms_norm(xc, g_norm2[l]), csh2, csc2)
            y = moe(jnp.concatenate([hx2, hc2], axis=1), w_router, b_router,
                    w_exp_gate[l], w_exp_up[l], w_exp_down[l])
            x = x + gt2 * y[:, :s]
            xc = xc + cgt2 * y[:, s:]
    return x


_drawn_inputs = setup_inputs


def setup_inputs(seed=0):
    import zlib

    import numpy as np

    out = dict(_drawn_inputs(seed))
    spreads = {}
    factors = {'g_norm1': 6.871,
     'q_norm': 33.255,
     'k_norm': 28.447,
     'hy_short_b': 8.0,
     'hy_b1': 8.0,
     'hy_b2': 8.0,
     'hy_freq': 8.0,
     'cf_dw_b': 47.52,
     'cf_ln_g': 64.0,
     'cf_ln_b': 55.976,
     'g_norm2': 8.0,
     'w_router': 3.449,
     'b_router': 8.0,
     'w_exp_gate': 3.375,
     'w_exp_up': 3.129,
     'w_exp_down': 3.145}
    for name, (base, spread) in spreads.items():
        noise = np.random.default_rng([zlib.crc32(name.encode()), seed]).standard_normal(out[name].shape)
        drawn = base * np.exp(spread * noise) if base else spread * noise
        out[name] = __import__('jax').numpy.asarray(drawn.astype(out[name].dtype))
    for name, factor in factors.items():
        out[name] = (out[name] * factor).astype(out[name].dtype)
    return out
```

```python
import math
from contextlib import ExitStack

import numpy as np
import concourse.bass as bass
from concourse import mybir


def shape_constants(seq, hyena_w):
    f = np.float32
    half, quarter = 32, 16
    t = np.arange(seq)
    inv = 10000.0 ** (-np.arange(0, half, 2) / half)
    row, col = (t // 64)[:, None] * inv, (t % 64)[:, None] * inv
    ang = np.concatenate([row, row, col, col], axis=-1).T
    cos, sin = np.cos(ang), np.sin(ang)
    rot = np.zeros((64, 64))
    for b in range(2):
        for i in range(quarter):
            rot[b * half + i, b * half + quarter + i] = -1.0
            rot[b * half + quarter + i, b * half + i] = 1.0
    rot2 = np.kron(np.eye(2), rot)
    theta = 2.0 * np.pi * (np.arange(seq) + 0.5) / (2 * seq)
    cc, ss = np.cos(np.outer(t, theta)), np.sin(np.outer(t, theta))
    tl = np.linspace(0.0, 1.0, seq)[:, None]
    w = 2.0 * np.pi * np.arange(seq)[:, None] / seq
    fr = np.linspace(1e-4, 15, 16)[None, :]
    feat = np.concatenate([tl, np.cos(fr * w), -np.sin(fr * w)], axis=-1)
    lo, hi = math.log(1e-2) / 1.5, math.log(1e-2) / 0.3
    deltas = np.tile(np.linspace(lo, hi, hyena_w), 2)
    decay = np.exp(-tl * np.abs(deltas))
    tile2 = lambda a: np.ascontiguousarray(a.reshape(2, 128, -1).transpose(1, 0, 2)).reshape(128, -1)
    i = np.arange(128)
    return {
        "c_ident": np.eye(128), "c_ones": np.ones((128, 128)),
        "c_headmean": np.kron(np.eye(2), np.ones((64, 64))) / 64.0,
        "c_before": (i[:, None] < i[None, :]), "c_iota": np.broadcast_to(i[None, :], (128, 128)),
        "c_rot": rot2.T, "c_headsum": np.kron(np.eye(2), np.ones((64, 1))),
        "c_fold": np.concatenate([np.eye(2), np.eye(2)]),
        "c_cos": np.concatenate([cos, cos]), "c_sin": np.concatenate([sin, sin]),
        "c_fwd": np.concatenate([tile2(cc), tile2(ss)], axis=1),
        "c_inv": np.concatenate([tile2(cc.T / seq), tile2(ss.T / seq)], axis=1),
        "c_feat": feat.T, "c_decay": tile2(decay),
        "c_first": np.broadcast_to(np.concatenate([16.0 - np.arange(16), 4.0 - np.arange(4), 1.0 + np.arange(16)])[None, :], (128, 36)),
    }, f


def hybrid_backbone(nc, A, out):
    f32, f32r, i32 = mybir.dt.float32, mybir.dt.float32r, mybir.dt.int32
    ALU, ACT, AX = mybir.AluOpType, mybir.ActivationFunctionType, mybir.AxisListType
    MUL, ADD, SUB = ALU.mult, ALU.add, ALU.subtract

    P = 128
    SEQ, D = A["x"].shape[1], A["x"].shape[2]
    DEPTH, NE, FF = A["w_mod"].shape[0], A["w_exp_gate"].shape[1], A["w_exp_gate"].shape[3]
    KT = D // P
    TOK = 2 * SEQ
    EPS = 1e-6
    UW = 256
    UE = KT * UW
    RING = 3
    BIG = 1.0e30
    NI = NE + (2 * TOK - 1) // P
    TWO_PI_HI, TWO_PI_LO, ROUND = 6.28125, 2 * math.pi - 6.28125, 1.5 * 2.0 ** 23
    PI = 3.1415925

    LAYER_SEMS = (
        "mean_sq", "root",
        "H_ok", "U", "Y", "aT", "a_hi", "a_lo", "act_a", "affin", "cf_mean", "cf_n", "cf_o",
        "cf_sq", "cf_var", "cf_xc", "comb0", "combT", "combined", "conv_ok", "e_hi", "e_lo",
        "e_used", "e_yev", "down_free", "ew0", "ew1", "ew2", "ew3", "ew4", "ew5", "ew6", "ew7", "ew8", "ew9", "ew10", "ew11",
        "exp", "f_abs", "f_arg", "f_mm", "f_raw", "f_sd", "f_sin",
        "g_hi", "g_lo", "gate_ok", "glu_free", "glu_ok", "h2", "h_hi", "h_lo", "hi",
        "hm", "hy_o", "k_g", "k_ok", "k_rot", "k_sq", "k_stat", "lo", "logits", "m_hi",
        "m_lo", "mg_a", "mg_c", "mg_h", "mod_done", "modcol", "moe_x", "n1_sq", "n1_stat", "n2_sq", "n2_stat", "nmax", "oa_hi", "oa_lo", "oc_hi", "oc_lo",
        "oh_hi", "oh_lo", "pT", "pT_act", "pT_dve", "pick", "pick_t", "places", "probs", "pv", "q_g", "q_ok", "q_rot", "q_sq", "q_stat", "items_ok", "routed", 
        "row_hi", "row_lo", "rows", "rows_ok", "score", "short", "silu", "tab_in", "u", "uT",
        "u_act", "u_dve", "v_ok", "vecT", "vec_ok", "vec_zero", "vrows", "w0", "w1", "w2",
        "x_moe", "xg_hi", "xg_lo", "y_hy", "y_out", "zf0", "zf1",
        "zr", "vec_in", "fil_in", "fil2_in", "spill",
    )

    units = [("mod", j) for j in range(8)]
    for j in range(8):
        units += [("in", j), ("mod", 8 + 2 * j), ("mod", 9 + 2 * j)]
    FIRST_GATE = len(units)
    units += [("gate", 4 + j) for j in range(4)] + [("proj_h", 0)]
    units += [("gate", j) for j in range(4)] + [("proj_a", 0), ("proj_a", 1)]
    units += [("gate", 8 + j) for j in range(4)] + [("proj_c", 0)]
    units += [("out", j) for j in range(4)]
    NU = len(units)
    at = {u: n for n, u in enumerate(units)}
    n_tiles = {"mod": 1, "in": 2, "gate": 2, "proj_h": 8, "proj_a": 4, "proj_c": 8, "out": 2}
    first_tile, total = [], 0
    for kind, _ in units:
        first_tile.append(total)
        total += n_tiles[kind]

    def unit_source(l, n):
        kind, j = units[n]
        if kind == "mod":
            return A["w_mod"][l, :, j * UW:(j + 1) * UW].rearrange("(k p) n -> p k n", p=P)
        if kind in ("in", "gate"):
            c = (j if kind == "in" else 8 + j) * UW
            return A["w_in"][l, :, c:c + UW].rearrange("(k p) n -> p k n", p=P)
        if kind == "proj_h":
            return A["p_hyena"][l].rearrange("(k p) n -> p k n", p=P)
        if kind == "proj_c":
            return A["p_conv"][l].rearrange("(k p) n -> p k n", p=P)
        if kind == "proj_a":
            return A["p_attn"][l, :, j * 512:(j + 1) * 512].rearrange("(k p) n -> p k n", p=P)
        return A["w_out"][l, :, j * UW:(j + 1) * UW].rearrange("(k p) n -> p k n", p=P)

    def unit_view(buf, n):
        k = {"proj_h": 2, "proj_c": 2, "proj_a": 4}.get(units[n][0], KT)
        return buf[:, :].rearrange("p (k n) -> p k n", k=k)

    HEAD0 = FIRST_GATE
    NH = 8

    ctx = ExitStack()
    with ctx:
        base = [-(-nc.sbuf_base // 64) * 64]
        LIMIT = nc.sbuf_usable_end

        def at_byte(name, shape, dt, off):
            size = 4 * int(np.prod(shape[1:]))
            assert off + size <= LIMIT, (name, off + size - LIMIT)
            return nc.alloc_sbuf_tensor_at(name, shape, dt, offset=off)

        def keep(name, shape, dt=f32):
            off = base[0]
            base[0] += -(-4 * int(np.prod(shape[1:])) // 32) * 32
            return at_byte(name, shape, dt, off)

        def region(kib):
            off = base[0]
            base[0] += int(kib * 1024)
            assert base[0] <= LIMIT, (base[0] - LIMIT)
            return off

        stage = [keep(f"stage{i}", [P, UE]) for i in range(RING)]
        whi = [keep(f"whi{i}", [P, UE], f32r) for i in range(RING)]
        wlo = [keep(f"wlo{i}", [P, UE], f32r) for i in range(RING)]
        ident, ones = keep("ident", [P, P]), keep("ones", [P, P])
        headmean, before = keep("headmean", [P, P]), keep("before", [P, P])
        iota, rot = keep("iota", [P, P]), keep("rot", [P, P])
        headsum, fold, first = keep("headsum", [P, 2]), keep("fold", [4, 2]), keep("first", [P, 36])
        cosT, sinT = keep("cosT", [P, SEQ]), keep("sinT", [P, SEQ])
        cst = keep("cst", [P, KT, P], f32r)
        NVEC1, NVEC2 = 99, 62
        vec = keep("vec", [P, NVEC1 + NVEC2])
        modT = keep("modT", [P, 96])
        amp = keep("amp", [P, 2, KT, 2])
        modrow = keep("modrow", [4, 2, UW])
        rsq = keep("rsq", [P, 4, NH])
        small = keep("small", [P, 32])
        router_b = keep("router_b", [P, NE])
        glu = keep("glu", [P, 2, 2, SEQ + 30])
        conv = keep("conv", [P, 2, TOK])
        R1, R2, R3, R4 = region(16), region(16), region(16), region(16)
        R5, R6, R7, R8 = region(8), region(8), region(8), region(8)
        R9, RK, RV = region(12), region(4), region(2)
        K = 1024
        xT = at_byte("xT", [P, KT, TOK], f32, R7)
        h_hi, h_lo = at_byte("h_hi", [P, KT, TOK], f32r, R1), at_byte("h_lo", [P, KT, TOK], f32r, R2)
        m_hi, m_lo = at_byte("m_hi", [P, KT, TOK], f32r, R1), at_byte("m_lo", [P, KT, TOK], f32r, R2)
        gates = at_byte("gates", [P, KT, TOK], f32, R3)
        merged = at_byte("merged", [P, KT, TOK], f32, R4)
        xrow = at_byte("xrow", [P, 4, D], f32, R4)
        vrow1, vrow2 = at_byte("vrow1", [P, P], f32, R5), at_byte("vrow2", [P, P], f32, R5 + 512)
        crow = at_byte("crow", [16, P], f32, R5 + 1024)
        crow_s = at_byte("crow_s", [16, P], f32, R5 + 1536)
        sq = at_byte("sq", [P, 2, TOK], f32, R5 + 2 * K)
        rs = at_byte("rs", [P, TOK], f32, R5 + 6 * K)
        hn = at_byte("hn", [P, 2, TOK], f32, R6)
        hm = at_byte("hm", [P, 2, TOK], f32, R6 + 4 * K)
        feat = at_byte("feat", [33, SEQ], f32, R3)
        fw1, fw2 = at_byte("fw1", [33, 64], f32, R3 + K), at_byte("fw2", [64, 64], f32, R3 + K + 256)
        fh = at_byte("fh", [64, 2, SEQ], f32, R3 + 2 * K)
        fw3 = at_byte("fw3", [64, 512], f32, R3 + 4 * K)
        hfil = at_byte("hfil", [P, 2, 512], f32, R3 + 6 * K)
        habs = at_byte("habs", [P, 2, 512], f32, R3 + 10 * K)
        hrow_d = at_byte("hrow_d", [1, SEQ], f32, R3 + 14 * K)
        decay = at_byte("decay", [P, 2, 512], f32, R4)
        fwd0 = at_byte("fwd0", [P, 2, 2, SEQ], f32, R4 + 4 * K)
        hinv = at_byte("hinv", [P, 512], f32, R4 + 8 * K)
        hs = at_byte("hs", [P, 2, SEQ], f32, R4 + 10 * K)
        hd = at_byte("hd", [P, 2, SEQ], f32, R4 + 12 * K)
        H = at_byte("H", [P, 2, 2, SEQ], f32, R9)
        zraw = at_byte("zraw", [P, 4, TOK], f32, R3)
        zsq = at_byte("zsq", [P, 4, TOK], f32, R3 + 8 * K)
        q = at_byte("q", [P, 4, TOK], f32, R5)
        kraw = at_byte("kraw", [P, TOK], f32, R6)
        ksq = at_byte("ksq", [P, TOK], f32, R6 + 2 * K)
        vT = at_byte("vT", [P, TOK], f32, R6 + 4 * K)
        krs = at_byte("krs", [P, TOK], f32, R6 + 6 * K)
        kd = at_byte("kd", [P, 2, TOK], f32, RK)
        vr = at_byte("vr", [P, 4, P], f32, RV)
        ropet = at_byte("ropet", [P, 2, SEQ], f32, R9 + 4 * K)
        zhy = at_byte("zhy", [P, 6, TOK], f32, R4)
        urow = at_byte("urow", [P, 2, TOK], f32, R7)
        fwd = at_byte("fwd", [P, 2, 2, SEQ], f32, R8)
        inv = at_byte("inv", [P, 2, 2, SEQ], f32, R8 + 4 * K)
        ytmp = at_byte("ytmp", [P, 2, TOK], f32, R3 + 8 * K)
        Y = at_byte("Y", [P, 2, 2, TOK], f32, R6)
        hyo = at_byte("hyo", [P, 2, TOK], f32, R3 + 8 * K)
        oh_hi, oh_lo = at_byte("oh_hi", [P, 2, TOK], f32r, R7), at_byte("oh_lo", [P, 2, TOK], f32r, R7 + 4 * K)
        gsig = at_byte("gsig", [P, 2, TOK], f32, R3 + 12 * K)
        probs = at_byte("probs", [P, 3, 512], f32, R9)
        pT = at_byte("pT", [P, 3, 512], f32, R9 + 6 * K)
        oa_hi, oa_lo = at_byte("oa_hi", [P, 4, TOK], f32r, R5), at_byte("oa_lo", [P, 4, TOK], f32r, R6)
        csq = at_byte("csq", [P, 2, TOK], f32, R9)
        crs = at_byte("crs", [P, TOK], f32, R9 + 4 * K)
        co = at_byte("co", [P, 2, TOK], f32, R9 + 6 * K)
        oc_hi, oc_lo = at_byte("oc_hi", [P, 2, TOK], f32r, R8), at_byte("oc_lo", [P, 2, TOK], f32r, R8 + 4 * K)
        t_hi, t_lo = at_byte("t_hi", [P, 4, D], f32r, R1), at_byte("t_lo", [P, 4, D], f32r, R2)
        h2T = at_byte("h2T", [P, KT, TOK], f32, R3)
        wr = at_byte("wr", [P, KT, NE], f32, R9)
        rt = at_byte("rt", [P, 14, 64], f32, R9 + 512)
        grp = at_byte("grp", [P, 8, 16], f32, R9 + 512 + 3584)
        posm = at_byte("posm", [P, 4, NI + 1], f32, R9 + 5 * K)
        tokv = at_byte("tokv", [P, 6, 4], f32, R9 + 5 * K + 512)
        rowid = at_byte("rowid", [P, 8], i32, R9 + 6 * K)
        chunks, starts = at_byte("chunks", [P, NE], f32, R9 + 6 * K + 64), at_byte("starts", [P, NE], f32, R9 + 6 * K + 128)
        ends = at_byte("ends", [P, 2, 8 + NE], f32, R9 + 6 * K + 192)
        item_base = at_byte("item_base", [P, NI + 1], f32, R9 + 6 * K + 384)
        item_f = at_byte("item_f", [P, NI], f32, R9 + 6 * K + 512)
        items_i = at_byte("items_i", [1, NI + 1], i32, R9 + 6 * K + 640)
        before_end = at_byte("before_end", [P, NI, NE], f32, R9 + 7 * K)
        zero_rows = at_byte("zero_rows", [P, D], f32, RK)
        xg_hi, xg_lo = at_byte("xg_hi", [P, KT, P], f32r, R4), at_byte("xg_lo", [P, KT, P], f32r, R4 + 4 * K)
        pick = at_byte("pick", [P, 4, P], f32r, R4 + 8 * K)
        act_s = at_byte("act_s", [P, FF], f32, R4 + 10 * K)
        act_a = at_byte("act_a", [P, FF], f32, R4 + 12 * K)
        a_hi, a_lo = at_byte("a_hi", [P, 4, P], f32r, R5), at_byte("a_lo", [P, 4, P], f32r, R5 + 2 * K)
        yrow = at_byte("yrow", [P, D], f32, R6 + 4 * K)
        HU, EW, EP = UE // 2, 12, 6
        stage_b = at_byte("stage_b", [P, 4 * HU], f32, R3)
        stage_c = at_byte("stage_c", [P, 2 * HU], f32, R5 + 4 * K)

        def half_unit(bufs, s):
            return bufs[s // 2][:, (s % 2) * HU:(s % 2 + 1) * HU]

        def estage(j):
            if j < 6:
                return half_unit(stage, j)
            return stage_b[:, (j - 6) * HU:(j - 5) * HU] if j < 10 else stage_c[:, (j - 10) * HU:(j - 9) * HU]

        yg = at_byte("yg", [P, 2, D], f32, R3)
        comb = at_byte("comb", [P, 2, D], f32, R3 + 8 * K)
        orow = at_byte("orow", [P, 2, D], f32, R4)

        bank = [ctx.enter_context(nc.psum_tensor(f"bank{i}", [P, 512], f32)) for i in range(8)]

        x_spill = nc.dram_tensor("x_spill", (P, KT * TOK), f32, kind="Internal").ap()
        y_rows = nc.dram_tensor("y_rows", ((NI + 1) * P, D), f32, kind="Internal").ap()

        sems = {name: ctx.enter_context(nc.semaphore(name)) for name in LAYER_SEMS}
        numbers = sorted(x.num for x in sems.values())
        assert numbers == list(range(numbers[0], numbers[0] + len(numbers)))

        def sem(l, name):
            if name in LAYER_SEMS:
                return sems[name]
            if (l, name) not in sems:
                sems[l, name] = ctx.enter_context(nc.semaphore(f"{name}_{l}"))
            return sems[l, name]

        class Program:

            def __init__(self, eng, name):
                self.eng, self.steps, self.count = eng, sem("all", name), 0

            def step(self, ins):
                self.count += 1
                ins.then_inc(self.steps, 1)

            def sync(self):
                self.eng.wait_ge(self.steps, self.count)

            def then(self, ins):
                self.step(ins)
                self.sync()

        block = ctx.enter_context(nc.Block())

        def span(l):
            return TOK if l < DEPTH - 1 else SEQ

        def seqs(l):
            return span(l) // SEQ

        @block.sync
        def _(sp):
            def load(l, name, dst, src):
                sp.dma_start(dst, src).then_inc(sem(l, name), 16)

            for name, t in (("c_ident", ident), ("c_ones", ones), ("c_headmean", headmean), ("c_before", before),
                            ("c_iota", iota), ("c_rot", rot), ("c_headsum", headsum), ("c_fold", fold),
                            ("c_first", first), ("c_cos", cosT), ("c_sin", sinT)):
                load("all", "const_in", t[:, :], A[name])
            for l in range(DEPTH):
                def unit(n):
                    if n >= RING:
                        sp.wait_ge(sem(l, "hi"), n - RING + 1)
                        sp.wait_ge(sem(l, "lo"), n - RING + 1)
                    sp.dma_start(unit_view(stage[n % RING], n), unit_source(l, n)).then_inc(sem(l, f"w{n % RING}"), 16)

                T = span(l)
                S = lambda name, l=l: sem(l, name)
                if l > 0:
                    sp.wait_ge(sem("all", "layer_done"), l)
                    sp.sem_inc(sem("all", "layer_begun"), 1)
                for n in range(NU):
                    unit(n)
                    if n == RING - 1:
                        if l == 0:
                            sp.wait_ge(sem("all", "xt_act"), 4)
                            sp.wait_ge(sem("all", "xt_dve"), 4)
                        load(l, "fil2_in", decay[:, :, :], A["c_decay"])
                        load(l, "fil2_in", fwd0[:, :, :, :], A["c_fwd"])
                        load(l, "spill", x_spill, xT[:, :, :].rearrange("p k n -> p (k n)"))
                    if l == 0 and n == at["in", 1]:
                        sp.wait_ge(sem("all", "zeros"), 1)
                        for b in range(NE + 1, NI + 1):
                            load("all", "y_zeroed", y_rows[b * P:(b + 1) * P, :], zero_rows[:, :])
                    if n == at["in", 3]:
                        sp.wait_ge(sem(l, "spill"), 16)
                        sp.wait_ge(sem(l, "h_lo"), KT)
                        load(l, "tab_in", fwd[:, :, :, :], A["c_fwd"])
                        load(l, "tab_in", inv[:, :, :, :], A["c_inv"])
                sp.wait_ge(sem(l, "lo"), NU)

                def expert_unit(e, i, j):
                    sp.wait_ge(S("e_lo"), i * EW + j + 1)
                    if j == 8:
                        sp.sem_inc(S("down_free"), 1)
                    w, r0, nr = ((A["w_exp_gate"], j % 4, 2 * P) if j < 4 else (A["w_exp_up"], j % 4, 2 * P) if j < 8
                                 else (A["w_exp_down"], j % 4, P))
                    src = w[l, bass.ds(e, 1), r0 * nr:(r0 + 1) * nr, :].rearrange("a (k p) n -> p (a k) n", p=P)
                    sp.dma_start(estage(j).rearrange("p (k n) -> p k n", k=nr // P), src).then_inc(S(f"ew{j}"), 16)

                def y_out(i):
                    sp.wait_ge(S("e_yev"), i + 1)
                    sp.dma_start(y_rows[bass.ds(i * P, P), :], yrow[:, :]).then_inc(S("y_out"), 16)

                def second_half(e, i):
                    for j in range(6, 10):
                        expert_unit(e, i, j)
                    y_out(i)
                    for j in range(10, EW):
                        expert_unit(e, i, j)

                for j in range(6):
                    expert_unit(0, 0, j)
                sp.wait_ge(S("rows"), 2 * (T // P))
                sp.wait_ge(S("items_ok"), 1)
                last = sp.value_load(items_i[0:1, NI:NI + 1], min_val=NE - 1, max_val=NI - 1)
                with sp.Fori(0, last) as i:
                    e = sp.value_load(items_i[0:1, bass.ds(i, 1)], min_val=0, max_val=NE - 1)
                    e_next = sp.value_load(items_i[0:1, bass.ds(i + 1, 1)], min_val=0, max_val=NE - 1)
                    second_half(e, i)
                    for j in range(6):
                        expert_unit(e_next, i + 1, j)
                second_half(NE - 1, last)
                y_out(last + 1)
                sp.sem_inc(sem("all", "engine_done"), 1)
                sp.wait_ge(sem("all", "layer_done"), l + 1)
            sp.wait_ge(sem("all", "rows_out"), 2 * 16)

        @block.gpsimd
        def _(pool):
            def load(l, name, dst, src):
                pool.dma_start(dst, src).then_inc(sem(l, name), 16)

            for l in range(DEPTH):
                T = span(l)
                S = lambda name, l=l: sem(l, name)
                if l > 0:
                    pool.wait_ge(sem("all", "layer_done"), l)
                    pool.sem_inc(sem("all", "layer_begun"), 1)
                pool.wait_ge(S("zr"), first_tile[at["out", 0]])
                pool.wait_ge(S("spill"), 16)
                load(l, "x_back", xT[:, :, :], x_spill)
                load(l, "x_back", wr[:, :, :], A["w_router"].rearrange("(k p) n -> p k n", p=P))
                if l == 0:
                    pool.wait_ge(sem("all", "y_zeroed"), (NI - NE) * 16)
                for t in range(T // P):
                    if t == 0:
                        pool.wait_ge(S("rows_ok"), 1)
                    else:
                        pool.wait_ge(S("combined"), t)
                    for c in range(2):
                        pool.indirect_dma_start(
                            out=yg[:, c, :], out_offset=None, in_=y_rows,
                            in_offset=bass.IndirectOffsetOnAxis(ap=rowid[:, 2 * t + c:2 * t + c + 1], axis=0),
                        ).then_inc(S(f"yg{c}"), 16)
                pool.sem_inc(sem("all", "engine_done"), 1)

        @block.scalar
        def _(act):
            a = Program(act, "act_steps")

            def fn(out_, in_, f, **kw):
                return nc.scalar.activation(out_, in_, f, **kw)

            def load(l, name, dst, src):
                act.dma_start(dst, src).then_inc(sem(l, name), 16)

            for l in range(DEPTH):
                T = span(l)
                NS = seqs(l)
                NF = 3 if NS == 2 else 2
                S = lambda name, l=l: sem(l, name)

                def split(n):
                    act.wait_ge(S(f"w{n % RING}"), 16 * (n // RING + 1))
                    if n >= RING:
                        act.wait_ge(S("zr"), first_tile[n - RING + 1])
                    fn(whi[n % RING][:, :], stage[n % RING][:, :], ACT.Copy).then_inc(S("hi"), 1)

                def tile_ready(m):
                    act.wait_ge(S("zr"), m + 1)

                def z(m):
                    return bank[m % 2]

                if l > 0:
                    act.wait_ge(sem("all", "layer_done"), l)
                    act.sem_inc(sem("all", "layer_begun"), 1)
                if l == 0:
                    load("all", "x_in", xrow[:, 0:2, :], A["x"][0].rearrange("(t p) n -> p t n", p=P))
                    load("all", "x_in", xrow[:, 2:4, :], A["ctx"][0].rearrange("(t p) n -> p t n", p=P))
                act.wait_ge(sem(l, "vec_zero"), 1)
                rows = [(0, A["b_mod"][l].rearrange("(r p) -> r p", p=P)), (48, A["g_norm1"][l].rearrange("(r p) -> r p", p=P)),
                        (56, A["g_norm2"][l].rearrange("(r p) -> r p", p=P)),
                        (64, A["hy_short_w"][l].rearrange("k (c p) -> (k c) p", p=P)),
                        (82, A["hy_short_b"][l].rearrange("(r p) -> r p", p=P)), (88, A["cf_dw_b"][l].rearrange("(r p) -> r p", p=P)),
                        (90, A["cf_ln_g"][l].rearrange("(r p) -> r p", p=P)), (92, A["cf_ln_b"][l].rearrange("(r p) -> r p", p=P))]
                for r0, src in rows:
                    load(l, "vec_in", vrow1[r0:r0 + src.shape[0], :], src)
                for r0, name in ((94, "q_norm"), (95, "k_norm")):
                    for h in range(2):
                        load(l, "vec_in", vrow1[r0:r0 + 1, 64 * h:64 * h + 64], A[name][l:l + 1, :])
                for r0, name in ((96, "hy_b1"), (97, "hy_b2"), (98, "hy_freq")):
                    load(l, "vec_in", vrow1[r0:r0 + 1, 0:64], A[name][l:l + 1, :])
                load(l, "vec_in", vrow2[0:NVEC2, :], A["cf_dw_w"][l].rearrange("k (c p) -> (k c) p", p=P))
                if l == 0:
                    load("all", "c_in", crow[0:8, :], A["c"].rearrange("a (r p) -> (a r) p", p=P))
                    load("all", "c_in", crow[8:16, :], A["c_ctx"].rearrange("(r p) -> r p", p=P))
                    load("all", "b_in", router_b[:, :], A["b_router"].rearrange("(a n) -> a n", a=1).to_broadcast([P, NE]))
                load(l, "fil_in", feat[:, :], A["c_feat"])
                load(l, "fil_in", fw1[:, :], A["hy_w1"][l])
                load(l, "fil_in", fw2[:, :], A["hy_w2"][l])
                load(l, "fil_in", fw3[:, :], A["hy_w3"][l])
                load(l, "fil_in", hrow_d[:, :], A["hy_bias"][l:l + 1, :])
                if l == 0:
                    act.wait_ge(sem("all", "c_in"), 32)
                    fn(crow_s[:, :], crow[:, :], ACT.Silu).then_inc(sem("all", "c_silu"), 1)
                    act.wait_ge(sem("all", "cT"), 1)
                    act.wait_ge(sem("all", "cst_zero"), 1)
                    fn(cst[:, :, 0:2], bank[1][:, 0:16].rearrange("p (s k) -> p k s", s=2), ACT.Copy).then_inc(sem("all", "c_hi"), 1)
                    for k in range(0, KT, 2):
                        act.wait_ge(sem("all", "xt"), k + 1)
                        fn(xT[:, k, :], bank[k][:, :], ACT.Copy).then_inc(sem("all", "xt_act"), 1)
                for k in range(KT):
                    if l == 0 and k % 2 == 0:
                        act.wait_ge(sem("all", "xt_act"), k // 2 + 1)
                    elif l == 0:
                        act.wait_ge(sem("all", "xt_dve"), k // 2 + 1)
                    if k >= 2:
                        act.wait_ge(S("n1_stat"), k - 1)
                    fn(sq[:, k % 2, :], xT[:, k, :], ACT.Square).then_inc(S("n1_sq"), 1)
                act.wait_ge(S("mean_sq"), 1)
                fn(rs[:, :], rs[:, :], ACT.Sqrt).then_inc(S("root"), 1)

                split(0)
                split(1)
                for n, (kind, j) in enumerate(units):
                    m = first_tile[n]
                    if n + 2 < NU:
                        split(n + 2)
                    if kind == "mod":
                        tile_ready(m)
                        if j >= 2:
                            act.wait_ge(S("modcol"), j - 1)
                        fn(modrow[:, j % 2, :], z(m)[0:4, 0:UW], ACT.Copy).then_inc(S(f"zf{m % 2}"), 1)
                    if n in (0, 1):
                        act.wait_ge(S("f_arg"), n + 1)
                        fn(fh[:, n, :], fh[:, n, :], ACT.Sin).then_inc(S("f_sin"), 1)
                    if n == 2:
                        for t in range(2):
                            act.wait_ge(S("f_raw"), t + 1)
                            fn(habs[:, t, :], hfil[:, t, :], ACT.Abs).then_inc(S("f_abs"), 1)
                    if n == 7:
                        for k in range(KT):
                            act.wait_ge(S("hm"), k + 1)
                            fn(h_hi[:, k, :], hm[:, k % 2, :], ACT.Copy).then_inc(S("h_hi"), 1)
                    if kind == "in" and j < 2:
                        for t in range(2):
                            i = 2 * j + t
                            tile_ready(m + t)
                            fn(zraw[:, i, 0:T], z(m + t)[:, 0:T], ACT.Copy).then_inc(S(f"zf{(m + t) % 2}"), 1)
                            act.wait_ge(S(f"zf{(m + t) % 2}"), (m + t) // 2 + 1)
                            fn(zsq[:, i, 0:T], zraw[:, i, 0:T], ACT.Square).then_inc(S("q_sq"), 1)
                    if n == at["mod", 11]:
                        act.wait_ge(S("mean_sq"), 2)
                        NQ = (T // P) * NH
                        fl = rsq[:, :, :].rearrange("p t h -> p (t h)")
                        fn(fl[:, 0:NQ], fl[:, 0:NQ], ACT.Sqrt).then_inc(S("root"), 1)
                    if kind == "in" and j == 2:
                        tile_ready(m)
                        fn(kraw[:, :], z(m)[:, :], ACT.Copy).then_inc(S(f"zf{m % 2}"), 1)
                        act.wait_ge(S(f"zf{m % 2}"), m // 2 + 1)
                        fn(ksq[:, :], kraw[:, :], ACT.Square).then_inc(S("k_sq"), 1)
                        tile_ready(m + 1)
                        fn(vT[:, :], z(m + 1)[:, :], ACT.Copy).then_inc(S(f"zf{(m + 1) % 2}"), 1)
                    if n == at["mod", 12]:
                        act.wait_ge(S("mean_sq"), 3)
                        fn(krs[:, :], krs[:, :], ACT.Sqrt).then_inc(S("root"), 1)
                        act.wait_ge(S("vrows"), 1)
                        fn(vr[:, :, :].rearrange("p t n -> p (t n)"), bank[5][:, :], ACT.Copy).then_inc(S("v_ok"), 1)
                    if kind == "in" and 3 <= j < 6:
                        for t in range(2):
                            i = 2 * (j - 3) + t
                            tile_ready(m + t)
                            if i >= 4:
                                act.wait_ge(S("short"), i - 3)
                            if i < 4:
                                act.wait_ge(S("q_ok"), 4)
                            fn(zraw[:, i % 4, 0:T], z(m + t)[:, 0:T], ACT.Copy).then_inc(S(f"zf{(m + t) % 2}"), 1)
                    if n == at["mod", 19]:
                        act.wait_ge(S("uT"), 1)
                        fn(urow[:, 0, 0:T], bank[5][:, 0:T], ACT.Copy).then_inc(S("u_act"), 1)
                    if kind == "in" and j >= 6:
                        for t in range(2):
                            tile_ready(m + t)
                            src = z(m + t)[:, 0:T].rearrange("p (s n) -> p s n", s=NS)
                            if j == 6:
                                act.wait_ge(S("glu_free"), 1)
                                fn(glu[:, t, 0:NS, 15:15 + SEQ], src, ACT.Copy).then_inc(S(f"zf{(m + t) % 2}"), 1)
                            else:
                                fn(gsig[:, t, 0:T], z(m + t)[:, 0:T], ACT.Sigmoid).then_inc(S(f"zf{(m + t) % 2}"), 1)
                    if n == at["mod", 23]:
                        for t in range(2):
                            act.wait_ge(S("hy_o"), t + 1)
                            fn(oh_hi[:, t, 0:T], hyo[:, t, 0:T], ACT.Copy).then_inc(S("oh_hi"), 1)

                    i = n - HEAD0
                    if 1 <= i <= NH:
                        act.wait_ge(S("pT"), NF * (i - 1) + 1)
                        if i >= 2:
                            act.wait_ge(S("pv"), i - 1)
                        fn(pT[:, 0, :], bank[5][:, :], ACT.Copy).then_inc(S("pT_act"), 1)
                    if kind == "gate":
                        for t in range(2):
                            tile_ready(m + t)
                            g = 2 * (j % 4) + t
                            if n < at["gate", 0] and j == 4 and t == 0:
                                act.wait_ge(S("glu_ok"), 2)
                                act.wait_ge(S("oh_lo"), 2)
                            if 0 <= j < 4:
                                act.wait_ge(S("mg_h"), g + 1)
                            if j >= 8:
                                act.wait_ge(S("mg_a"), g + 1)
                            fn(gates[:, g, 0:T], z(m + t)[:, 0:T], ACT.Copy).then_inc(S(f"zf{(m + t) % 2}"), 1)
                    if 1 <= i <= NH and NS == 2:
                        act.wait_ge(S("pT"), NF * i)
                        fn(pT[:, 2, :], bank[5][:, :], ACT.Copy).then_inc(S("pT_act"), 1)
                    if 0 <= i < NH:
                        act.wait_ge(S("nmax"), i + 1)
                        if i >= 1:
                            act.wait_ge(S("pT"), NF * i)
                        for c in range(T // P):
                            src = bank[2 + c][:, :] if c < 2 else bank[4][:, (c - 2) * 256:(c - 1) * 256]
                            dst = probs[:, c, :] if c < 2 else probs[:, 2, (c - 2) * 256:(c - 1) * 256]
                            ins = fn(dst, src, ACT.Exp, bias=small[:, 4 + c:5 + c], scale=rsq[:, c, i:i + 1],
                                     accum_out=small[:, 8 + c:9 + c])
                            ins.then_inc(S("exp"), 1)
                    if 1 <= i <= NH:
                        if i % 2 == 0:
                            act.wait_ge(S("pv"), i)
                            fn(oa_hi[:, i // 2 - 1, 0:T], bank[7][:, 0:T], ACT.Copy).then_inc(S("oa_hi"), 1)
                    if n in (at["gate", 7], at["gate", 3], at["gate", 11]):
                        act.wait_ge(S(f"zf{(m + 1) % 2}"), (m + 1) // 2 + 1)
                        act.wait_ge(S(f"zf{m % 2}"), m // 2 + 1)
                        fn(gates[:, :, 0:T], gates[:, :, 0:T], ACT.Sigmoid).then_inc(S("gate_ok"), 1)
                    if n == at["gate", 8]:
                        for t in range(2):
                            act.wait_ge(S("cf_xc"), t + 1)
                            fn(csq[:, t, 0:T], conv[:, t, 0:T], ACT.Square).then_inc(S("cf_sq"), 1)
                    if n == at["gate", 9]:
                        act.wait_ge(S("mean_sq"), 4)
                        fn(crs[:, 0:T], crs[:, 0:T], ACT.Sqrt).then_inc(S("root"), 1)
                    if n == at["gate", 10]:
                        for t in range(2):
                            act.wait_ge(S("cf_n"), t + 1)
                            fn(co[:, t, 0:T], conv[:, t, 0:T], ACT.Silu, scale=vec[:, 90 + t:91 + t],
                               bias=vec[:, 92 + t:93 + t]).then_inc(S("cf_o"), 1)
                            act.wait_ge(S("cf_o"), t + 1)
                            fn(oc_hi[:, t, 0:T], co[:, t, 0:T], ACT.Copy).then_inc(S("oc_hi"), 1)
                    if kind == "proj_c":
                        for t in range(KT):
                            act.wait_ge(S("mg_c"), t + 1)
                            fn(m_hi[:, t, 0:T], merged[:, t, 0:T], ACT.Copy).then_inc(S("m_hi"), 1)

                for k in range(KT):
                    mk = first_tile[at["out", 0]] + k
                    act.wait_ge(S(f"zf{mk % 2}"), mk // 2 + 1)
                    if k >= 2:
                        act.wait_ge(S("n2_stat"), k - 1)
                    fn(sq[:, k % 2, 0:T], xT[:, k, 0:T], ACT.Square).then_inc(S("n2_sq"), 1)
                act.wait_ge(S("mean_sq"), 5)
                fn(rs[:, 0:T], rs[:, 0:T], ACT.Sqrt).then_inc(S("root"), 1)
                NT = T // P
                act.wait_ge(S("logits"), 1)
                fn(rt[:, 0, 0:NT * NE], bank[0][:, 0:NT * NE], ACT.Sigmoid).then_inc(S("affin"), 1)
                for t in range(NT):
                    for c in range(2):
                        b = 2 * t + c
                        act.wait_ge(S("rows"), b + 1)
                        fn(t_hi[:, t, c * 512:(c + 1) * 512], bank[b][:, :], ACT.Copy).then_inc(S("row_hi"), 1)

                act.wait_ge(S("hi"), NU)
                act.wait_ge(S("zr"), total)
                act.sem_inc(S("e_hi"), EW)
                act.sem_inc(S("y_out"), 16)
                def esplit(i, j):
                    act.wait_ge(S(f"ew{j}"), (i + 1) * 16)
                    act.wait_ge(S("e_used"), i * EW + j + 1)
                    fn(half_unit(whi, j % EP), estage(j), ACT.Copy).then_inc(S("e_hi"), 1)

                def gathered(i):
                    act.wait_ge(S("e_used"), i * EW - 4 + EP)
                    for c in range(2):
                        act.wait_ge(S("g_hi"), i * 2 + c + 1)
                        fn(xg_hi[:, 4 * c:4 * c + 4, :].rearrange("p k n -> p (k n)"), bank[2 + c][:, :], ACT.Copy).then_inc(S("xg_hi"), 1)

                def y_evac(i):
                    act.wait_ge(S("y_out"), i * 16 + 16)
                    act.wait_ge(S("e_used"), i * EW + EP)
                    for c in range(2):
                        ins = fn(yrow[:, c * 512:(c + 1) * 512], bank[6 + c][:, :], ACT.Copy)
                    ins.then_inc(S("e_yev"), 1)

                def item(i, more):
                    y_evac(i)
                    for j in range(6, 10):
                        esplit(i, j)
                    act.wait_ge(S("e_used"), i * EW + 4 + EP)
                    fn(act_s[:, :], bank[0][:, :], ACT.Silu).then_inc(S("silu"), 1)
                    esplit(i, 10)
                    esplit(i, 11)
                    if more:
                        esplit(i + 1, 0)
                        gathered(i + 1)
                    act.wait_ge(S("aT"), i + 1)
                    fn(a_hi[:, :, :].rearrange("p k n -> p (k n)"), bank[0][:, :], ACT.Copy).then_inc(S("a_hi"), 1)
                    if more:
                        for j in range(1, 6):
                            esplit(i + 1, j)

                for j in range(6):
                    esplit(0, j)
                act.wait_ge(S("items_ok"), 1)
                last = act.value_load(items_i[0:1, NI:NI + 1], min_val=NE - 1, max_val=NI - 1)
                gathered(0)
                with act.Fori(0, last) as i:
                    item(i, True)
                item(last, False)
                y_evac(last + 1)
                act.sem_inc(sem("all", "engine_done"), 1)
                if l == DEPTH - 1:
                    for t in range(2):
                        act.wait_ge(sem("all", "orow_ok"), 2 * (t + 1))
                        act.dma_start(out[0, t * P:(t + 1) * P, :], orow[:, t, :]).then_inc(sem("all", "rows_out"), 16)
                    act.wait_ge(sem("all", "rows_out"), 32)

        @block.vector
        def _(dve):
            v = Program(dve, "dve_steps")
            V = nc.vector

            def tt(o, x, y, op):
                return V.tensor_tensor(o, x, y, op)

            def ts(o, x, s1, s2, op0, op1=None):
                return V.tensor_scalar(o, x, s1, s2, op0, op1) if op1 is not None else V.tensor_scalar(o, x, s1, None, op0)

            def stt(o, x, s, y, op0, op1):
                return V.scalar_tensor_tensor(out=o, in0=x, scalar=s, in1=y, op0=op0, op1=op1)

            V.memset(cst[:, :, :].bitcast(f32), 0.0).then_inc(sem("all", "cst_zero"), 1)
            V.memset(zero_rows[:, :], 0.0).then_inc(sem("all", "zeros"), 1)
            v.then(V.memset(glu[:, :, :, :], 0.0))
            dve.wait_ge(sem("all", "const_in"), 11 * 16)
            for l in range(DEPTH):
                T = span(l)
                NS = seqs(l)
                NF = 3 if NS == 2 else 2
                NT = T // P
                S = lambda name, l=l: sem(l, name)

                def split(n):
                    dve.wait_ge(S("hi"), n + 1)
                    if n >= RING:
                        dve.wait_ge(S("zr"), first_tile[n - RING + 1])
                    tt(wlo[n % RING][:, :], stage[n % RING][:, :], whi[n % RING][:, :].bitcast(f32), SUB).then_inc(S("lo"), 1)

                def tile_ready(m):
                    dve.wait_ge(S("zr"), m + 1)

                def z(m):
                    return bank[m % 2]

                def vcol(c):
                    return vec[:, c:c + 1]

                def modulation(half):
                    lo_, hi_ = (0, 32) if half == 0 else (32, 96)
                    dve.wait_ge(S("modcol"), 8 if half == 0 else 24)
                    b = vec[:, lo_ // 2:hi_ // 2].unsqueeze(2).to_broadcast([P, (hi_ - lo_) // 2, 2])
                    v.then(tt(modT[:, lo_:hi_].rearrange("p (c s) -> p c s", s=2), bank[7][:, lo_:hi_].rearrange("p (c s) -> p c s", s=2), b, ADD))
                    sc = (16, 64)[half]
                    g = vec[:, 48 + 8 * half:56 + 8 * half].unsqueeze(2).to_broadcast([P, KT, 2])
                    src = modT[:, sc:sc + 16].rearrange("p (k s) -> p k s", s=2)
                    v.then(ts(amp[:, half, :, :], src, 1.0, None, ADD))
                    v.then(tt(amp[:, half, :, :], amp[:, half, :, :], g, MUL))

                def shift(chunk, k, s):
                    c = chunk * 16 + 2 * k + s
                    return modT[:, c:c + 1]

                def inverse_rms(stat, name, T_, bnk):
                    dve.wait_ge(S(f"{name}_stat"), KT)
                    ts(rs[:, 0:T_], bnk[:, 0:T_], 1.0 / D, EPS, MUL, ADD).then_inc(S("mean_sq"), 1)
                    dve.wait_ge(S("root"), 1 if name == "n1" else 5)
                    v.then(V.reciprocal(rs[:, 0:T_], rs[:, 0:T_]))

                if l > 0:
                    dve.wait_ge(sem("all", "layer_done"), l)
                    dve.sem_inc(sem("all", "layer_begun"), 1)
                dve.sem_inc(S("glu_free"), 1)
                v.then(V.memset(vrow1[:, :], 0.0))
                V.memset(vrow2[:, :], 0.0).then_inc(S("vec_zero"), 1)
                dve.wait_ge(S("vecT"), 1)
                V.tensor_copy(vec[:, :], bank[0][:, 0:NVEC1 + NVEC2]).then_inc(S("vec_ok"), 1)
                if l == 0:
                    dve.wait_ge(sem("all", "c_hi"), 1)
                    tt(cst[:, :, 2:4], bank[1][:, 0:16].rearrange("p (s k) -> p k s", s=2), cst[:, :, 0:2].bitcast(f32), SUB).then_inc(sem("all", "c_lo"), 1)
                    for k in range(1, KT, 2):
                        dve.wait_ge(sem("all", "xt"), k + 1)
                        V.tensor_copy(xT[:, k, :], bank[k][:, :]).then_inc(sem("all", "xt_dve"), 1)
                inverse_rms(None, "n1", TOK, bank[2])

                def sine_argument(i):
                    dve.wait_ge(S("f_mm"), i + 1)
                    dve.wait_ge(S("vec_ok"), 1)
                    f, n_ = fh[:, i, :], habs[0:64, 0, 0:SEQ]
                    v.then(ts(f, bank[3][0:64, 0:SEQ], vec[0:64, 96 + i:97 + i], vec[0:64, 98:99], ADD, MUL))
                    v.then(ts(n_, f, 1.0 / (2 * math.pi), ROUND, MUL, ADD))
                    v.then(ts(n_, n_, ROUND, None, SUB))
                    v.then(stt(f, n_, -TWO_PI_HI, f, MUL, ADD))
                    v.then(stt(f, n_, -TWO_PI_LO, f, MUL, ADD))
                    ts(f, f, PI, -PI, ALU.min, ALU.max).then_inc(S("f_arg"), 1)

                def taps(k0, k1):
                    for k in range(k0, min(k1, 31)):
                        for t in range(2):
                            src = glu[:, t, 0:NS, k:k + SEQ]
                            dst = conv[:, t, 0:T].rearrange("p (s n) -> p s n", s=NS)
                            w = vcol(NVEC1 + 2 * k + t)
                            if k == 0:
                                v.step(ts(dst, src, w, vcol(88 + t), MUL, ADD))
                            else:
                                dve.wait_ge(v.steps, v.count - 1)
                                v.step(stt(dst, src, w, dst, MUL, ADD))
                    v.sync()

                split(0)
                split(1)
                taps_done = 0
                for n, (kind, j) in enumerate(units):
                    m = first_tile[n]
                    if n + 2 < NU:
                        split(n + 2)
                    if n in (0, 1):
                        sine_argument(n)
                    if n == 2:
                        dve.wait_ge(S("fil2_in"), 32)
                        for t in range(2):
                            dve.wait_ge(S("f_mm"), 3 + t)
                            tt(hfil[:, t, :], bank[4 + t][:, :], decay[:, t, :], MUL).then_inc(S("f_raw"), 1)
                    if n == 3:
                        dve.wait_ge(S("f_mm"), 5)
                        v.then(V.reciprocal(hinv[:, :], bank[6][:, :]))
                        for t in range(2):
                            v.then(tt(hfil[:, t, :], hfil[:, t, :], hinv[:, :], MUL))
                        v.then(V.memset(hfil[0:1, 0, SEQ:2 * SEQ], 0.0))
                        v.step(tt(hs[:, :, :], hfil[:, :, 0:SEQ], hfil[:, :, SEQ:2 * SEQ], ADD))
                        tt(hd[:, :, :], hfil[:, :, 0:SEQ], hfil[:, :, SEQ:2 * SEQ], SUB).then_inc(S("f_sd"), 1)
                    if n == 4:
                        dve.wait_ge(S("f_mm"), 6)
                        v.step(V.tensor_copy(H[:, 0, :, :].rearrange("p f n -> p (f n)"), bank[3][:, :]))
                        V.tensor_copy(H[:, 1, :, :].rearrange("p f n -> p (f n)"), bank[4][:, :]).then_inc(S("H_ok"), 1)
                    if n == 7:
                        modulation(0)
                        for k in range(KT):
                            if k >= 2:
                                dve.wait_ge(S("h_hi"), k - 1)
                                dve.wait_ge(S("h_lo"), k - 1)
                            v.then(tt(hn[:, k % 2, :], xT[:, k, :], rs[:, :], MUL))
                            ins = None
                            for s in range(2):
                                ins = ts(hm[:, k % 2, s * SEQ:(s + 1) * SEQ], hn[:, k % 2, s * SEQ:(s + 1) * SEQ],
                                         amp[:, 0, k, s:s + 1], shift(0, k, s), MUL, ADD)
                                if s == 0:
                                    v.step(ins)
                            ins.then_inc(S("hm"), 1)
                            dve.wait_ge(S("h_hi"), k + 1)
                            tt(h_lo[:, k, :], hm[:, k % 2, :], h_hi[:, k, :].bitcast(f32), SUB).then_inc(S("h_lo"), 1)
                    if kind == "in" and j < 2:
                        for t in range(2):
                            i = 2 * j + t
                            dve.wait_ge(S(f"zf{(m + t) % 2}"), (m + t) // 2 + 1)
                            if i == 0:
                                dve.wait_ge(S("h_lo"), KT)
                            ts(q[:, i, 0:T], zraw[:, i, 0:T], vcol(94), None, MUL).then_inc(S("q_g"), 1)
                    if n == at["mod", 11]:
                        dve.wait_ge(S("q_stat"), 1)
                        NQ = NT * NH
                        fl = rsq[:, :, :].rearrange("p t h -> p (t h)")
                        ts(fl[:, 0:NQ], bank[6][:, 0:NQ], 1.0, 64.0 * EPS, MUL, ADD).then_inc(S("mean_sq"), 1)
                        dve.wait_ge(S("root"), 2)
                        v.then(V.reciprocal(fl[:, 0:NQ], fl[:, 0:NQ]))
                        for i in range(4):
                            dve.wait_ge(S("q_rot"), 4)
                            dve.wait_ge(S("q_g"), i + 1)
                            v.then(tt(ropet[:, i % 2, :], bank[2 + i // 2][:, (i % 2) * SEQ:(i % 2 + 1) * SEQ], sinT[:, :], MUL))
                            v.then(tt(q[:, i, 0:SEQ], q[:, i, 0:SEQ], cosT[:, :], MUL))
                            tt(q[:, i, 0:SEQ], q[:, i, 0:SEQ], ropet[:, i % 2, :], ADD).then_inc(S("q_ok"), 1)
                    if n == at["mod", 12]:
                        dve.wait_ge(S("k_stat"), 1)
                        ts(krs[:, :], bank[4][:, :], EPS, None, ADD).then_inc(S("mean_sq"), 1)
                        dve.wait_ge(S("root"), 3)
                        v.then(V.reciprocal(krs[:, :], krs[:, :]))
                        v.then(tt(kraw[:, :], kraw[:, :], krs[:, :], MUL))
                        ts(kraw[:, :], kraw[:, :], vcol(95), None, MUL).then_inc(S("k_g"), 1)
                    if n == at["mod", 13]:
                        dve.wait_ge(S("k_rot"), 1)
                        v.then(tt(ropet[:, 0, :], bank[4][:, 0:SEQ], sinT[:, :], MUL))
                        v.then(tt(kraw[:, 0:SEQ], kraw[:, 0:SEQ], cosT[:, :], MUL))
                        v.then(tt(kraw[:, 0:SEQ], kraw[:, 0:SEQ], ropet[:, 0, :], ADD))
                        if l == 0:
                            dve.wait_ge(sem("all", "y_zeroed"), (NI - NE) * 16)
                        for g in range(2):
                            for h in range(2):
                                ins = V.tensor_copy(kd[64 * h:64 * h + 64, g, :], kraw[64 * g:64 * g + 64, :])
                                if (g, h) != (1, 1):
                                    v.step(ins)
                        ins.then_inc(S("k_ok"), 1)
                    if kind == "in" and 3 <= j < 6:
                        for t in range(2):
                            i = 2 * (j - 3) + t
                            dve.wait_ge(S(f"zf{(m + t) % 2}"), (m + t) // 2 + 1)
                            src = zraw[:, i % 4, 0:T].rearrange("p (s n) -> p s n", s=NS)
                            dst = zhy[:, i, 0:T].rearrange("p (s n) -> p s n", s=NS)
                            v.then(ts(dst, src, vcol(64 + 6 + i), vcol(82 + i), MUL, ADD))
                            v.then(stt(dst[:, :, 1:SEQ], src[:, :, 0:SEQ - 1], vcol(64 + i), dst[:, :, 1:SEQ], MUL, ADD))
                            stt(dst[:, :, 0:SEQ - 1], src[:, :, 1:SEQ], vcol(64 + 12 + i), dst[:, :, 0:SEQ - 1], MUL, ADD).then_inc(S("short"), 1)
                        if j == 5:
                            for t in range(2):
                                dve.wait_ge(S("short"), 5 + t)
                                tt(zhy[:, 2 + t, 0:T], zhy[:, 4 + t, 0:T], zhy[:, 2 + t, 0:T], MUL).then_inc(S("u"), 1)
                    if n == at["mod", 19]:
                        dve.wait_ge(S("uT"), 2)
                        V.tensor_copy(urow[:, 1, 0:T], bank[6][:, 0:T]).then_inc(S("u_dve"), 1)
                    if n == at["in", 6]:
                        for f in range(2):
                            dve.wait_ge(S("U"), 2 * (f + 1))
                            ur, ui = bank[2 + 2 * f], bank[3 + 2 * f]
                            for s in range(NS):
                                c = slice(s * SEQ, (s + 1) * SEQ)
                                v.step(tt(ytmp[:, 0, c], ur[:, c], H[:, 0, f, :], MUL))
                                v.then(tt(ytmp[:, 1, c], ui[:, c], H[:, 1, f, :], MUL))
                                v.then(tt(Y[:, 0, f, c], ytmp[:, 0, c], ytmp[:, 1, c], SUB))
                                v.step(tt(ytmp[:, 0, c], ur[:, c], H[:, 1, f, :], MUL))
                                v.then(tt(ytmp[:, 1, c], ui[:, c], H[:, 0, f, :], MUL))
                                tt(Y[:, 1, f, c], ytmp[:, 0, c], ytmp[:, 1, c], ADD).then_inc(S("Y"), 1)
                                dve.wait_ge(S("Y"), f * NS + s + 1)
                    if n == at["in", 7]:
                        for t in range(2):
                            dve.wait_ge(S(f"zf{(m + t) % 2}"), (m + t) // 2 + 1)
                            g = glu[:, t, 0:NS, 15:15 + SEQ]
                            tt(g, g, gsig[:, t, 0:T].rearrange("p (s n) -> p s n", s=NS), MUL).then_inc(S("glu_ok"), 1)
                        dve.wait_ge(S("glu_ok"), 2)
                    if n == at["mod", 23]:
                        for t in range(2):
                            dve.wait_ge(S("y_hy"), t + 1)
                            tt(hyo[:, t, 0:T], bank[5 + t][:, 0:T], zhy[:, t, 0:T], MUL).then_inc(S("hy_o"), 1)
                            dve.wait_ge(S("oh_hi"), t + 1)
                            tt(oh_lo[:, t, 0:T], hyo[:, t, 0:T], oh_hi[:, t, 0:T].bitcast(f32), SUB).then_inc(S("oh_lo"), 1)
                        modulation(1)
                        dve.sem_inc(S("mod_done"), 1)

                    if kind in ("proj_h", "proj_a", "proj_c"):
                        dve.wait_ge(S("gate_ok"), {"proj_h": 1, "proj_a": 2, "proj_c": 3}[kind])
                        for t in range(n_tiles[kind]):
                            g = 4 * j + t
                            tile_ready(m + t)
                            zt = z(m + t)[:, 0:T]
                            free = S(f"zf{(m + t) % 2}")
                            if kind == "proj_h":
                                tt(merged[:, g, 0:T], gates[:, g, 0:T], zt, MUL).then_inc(free, 1)
                                dve.wait_ge(free, (m + t) // 2 + 1)
                                dve.sem_inc(S("mg_h"), 1)
                            else:
                                tt(gates[:, g, 0:T], gates[:, g, 0:T], zt, MUL).then_inc(free, 1)
                                dve.wait_ge(free, (m + t) // 2 + 1)
                                tt(merged[:, g, 0:T], merged[:, g, 0:T], gates[:, g, 0:T], ADD).then_inc(S("mg_a" if kind == "proj_a" else "mg_c"), 1)
                            if kind == "proj_c" and t >= 1:
                                dve.wait_ge(S("m_hi"), t)
                                tt(m_lo[:, t - 1, 0:T], merged[:, t - 1, 0:T], m_hi[:, t - 1, 0:T].bitcast(f32), SUB).then_inc(S("m_lo"), 1)
                        if kind == "proj_c":
                            dve.wait_ge(S("m_hi"), KT)
                            tt(m_lo[:, KT - 1, 0:T], merged[:, KT - 1, 0:T], m_hi[:, KT - 1, 0:T].bitcast(f32), SUB).then_inc(S("m_lo"), 1)
                    i = n - HEAD0
                    if 1 <= i <= NH:
                        dve.wait_ge(S("pT"), NF * (i - 1) + 2)
                        if i >= 2:
                            dve.wait_ge(S("pv"), i - 1)
                        V.tensor_copy(pT[:, 1, :], bank[6][:, :]).then_inc(S("pT_dve"), 1)
                    if 0 <= i < NH:
                        dve.wait_ge(S("score"), i + 1)
                        v.step(V.reduce_max(small[:, 0:1], bank[2][:, :], AX.X))
                        v.step(V.reduce_max(small[:, 1:2], bank[3][:, :], AX.X))
                        if NS == 2:
                            v.step(V.reduce_max(small[:, 2:4], bank[4][:, :].rearrange("p (c n) -> p c n", c=2), AX.X))
                        v.sync()
                        stt(small[:, 4:4 + NT], small[:, 0:NT], -1.0, rsq[:, 0:NT, i], MUL, MUL).then_inc(S("nmax"), 1)
                        dve.wait_ge(S("exp"), NT * (i + 1))
                        v.then(V.reciprocal(small[:, 12:12 + NT], small[:, 8:8 + NT]))
                        for c in range(NT):
                            p_ = probs[:, c, :] if c < 2 else probs[:, 2, (c - 2) * 256:(c - 1) * 256]
                            ts(p_, p_, small[:, 12 + c:13 + c], None, MUL).then_inc(S("probs"), 1)
                    if 1 <= i <= NH and i % 2 == 0:
                        dve.wait_ge(S("oa_hi"), i // 2)
                        tt(oa_lo[:, i // 2 - 1, 0:T], bank[7][:, 0:T], oa_hi[:, i // 2 - 1, 0:T].bitcast(f32), SUB).then_inc(S("oa_lo"), 1)
                    if at["in", 7] <= n < at["gate", 8] and taps_done < 31:
                        more = 2 if n < FIRST_GATE else 4
                        taps(taps_done, taps_done + more)
                        taps_done = min(31, taps_done + more)
                        if taps_done == 31:
                            dve.sem_inc(S("conv_ok"), 1)
                    if n == at["gate", 8]:
                        dve.wait_ge(S("cf_mean"), 1)
                        for t in range(2):
                            stt(conv[:, t, 0:T], bank[5][:, 0:T], -1.0 / 256, conv[:, t, 0:T], MUL, ADD).then_inc(S("cf_xc"), 1)
                    if n == at["gate", 9]:
                        dve.wait_ge(S("cf_var"), 1)
                        ts(crs[:, 0:T], bank[6][:, 0:T], 1.0 / 256, EPS, MUL, ADD).then_inc(S("mean_sq"), 1)
                        dve.wait_ge(S("root"), 4)
                        v.then(V.reciprocal(crs[:, 0:T], crs[:, 0:T]))
                        for t in range(2):
                            tt(conv[:, t, 0:T], conv[:, t, 0:T], crs[:, 0:T], MUL).then_inc(S("cf_n"), 1)
                    if n == at["gate", 10]:
                        for t in range(2):
                            dve.wait_ge(S("oc_hi"), t + 1)
                            tt(oc_lo[:, t, 0:T], co[:, t, 0:T], oc_hi[:, t, 0:T].bitcast(f32), SUB).then_inc(S("oc_lo"), 1)
                    if kind == "out":
                        dve.wait_ge(S("x_back"), 32)
                        for t in range(2):
                            k = 2 * j + t
                            tile_ready(m + t)
                            for s in range(NS):
                                c = slice(s * SEQ, (s + 1) * SEQ)
                                ins = stt(xT[:, k, c], z(m + t)[:, c], shift(2, k, s), xT[:, k, c], MUL, ADD)
                                if s < NS - 1:
                                    v.step(ins)
                            ins.then_inc(S(f"zf{(m + t) % 2}"), 1)

                inverse_rms(None, "n2", T, bank[2])
                for k in range(KT):
                    if k >= 2:
                        dve.wait_ge(S("h2"), k - 1)
                    v.then(tt(hn[:, k % 2, 0:T], xT[:, k, 0:T], rs[:, 0:T], MUL))
                    for s in range(NS):
                        c = slice(s * SEQ, (s + 1) * SEQ)
                        ins = ts(h2T[:, k, c], hn[:, k % 2, c], amp[:, 1, k, s:s + 1], shift(3, k, s), MUL, ADD)
                        if s < NS - 1:
                            v.step(ins)
                    ins.then_inc(S("h2"), 1)

                W = NT * NE
                dve.wait_ge(sem("all", "b_in"), 16)
                dve.wait_ge(S("affin"), 1)
                aff = rt[:, 0, 0:W]
                e3 = lambda x: x.rearrange("p (t e) -> p t e", e=NE)
                row = lambda i: rt[:, i, 0:W]
                gr = lambda i: grp[:, i, 0:NT * 4]
                sel = row(1)
                v.then(tt(e3(sel), e3(aff), router_b[:, :].unsqueeze(1).to_broadcast([P, NT, NE]), ADD))
                s4 = sel.rearrange("p (g e) -> p g e", e=4)
                a0, a1, a2, a3 = (s4[:, :, c] for c in range(4))
                v.step(tt(gr(0), a0, a1, ALU.max))
                v.step(tt(gr(1), a0, a1, ALU.min))
                v.step(tt(gr(2), a2, a3, ALU.max))
                v.then(tt(gr(3), a2, a3, ALU.min))
                v.step(tt(gr(4), gr(0), gr(2), ALU.max))
                v.step(tt(gr(5), gr(0), gr(2), ALU.min))
                v.then(tt(gr(6), gr(1), gr(3), ALU.max))
                v.then(tt(gr(5), gr(5), gr(6), ALU.max))
                v.then(tt(gr(4), gr(4), gr(5), ADD))
                g3 = lambda x: x.rearrange("p (t g) -> p t g", g=4)

                def pick_first(values, width, order, key, best, view):
                    v.then(V.reduce_max(best, view(values), AX.X))
                    bb = best.unsqueeze(2).to_broadcast([P, NT, width])
                    v.then(tt(view(key), view(values), bb, ALU.is_equal))
                    oo = order.unsqueeze(1).to_broadcast([P, NT, width])
                    v.then(tt(view(key), view(key), oo, MUL))
                    v.then(V.reduce_max(best, view(key), AX.X))
                    v.then(tt(view(key), view(key), bb, ALU.is_equal))

                pick_first(gr(4), 4, first[:, 16:20], gr(6), tokv[:, 0, 0:NT], g3)
                v.then(ts(gr(7), gr(6), 1.0, BIG, SUB, MUL))
                inside = gr(6).unsqueeze(2).to_broadcast([P, NT * 4, 4])
                outside = gr(7).unsqueeze(2).to_broadcast([P, NT * 4, 4])
                m4 = row(2).rearrange("p (g e) -> p g e", e=4)
                v.then(tt(m4, s4, inside, MUL))
                v.then(tt(m4, m4, outside, ADD))
                pick_first(row(2), NE, first[:, 0:16], row(3), tokv[:, 0, 0:NT], e3)
                v.then(stt(row(2), row(3), -BIG, row(2), MUL, ADD))
                pick_first(row(2), NE, first[:, 0:16], row(4), tokv[:, 0, 0:NT], e3)
                tt(row(5), row(3), row(4), ADD).then_inc(S("routed"), 1)
                dve.wait_ge(S("routed"), 1)
                for c in range(2):
                    v.then(tt(row(6), aff, row(3 + c), MUL))
                    v.then(V.reduce_sum(tokv[:, 1 + c, 0:NT], e3(row(6)), AX.X))
                v.then(tt(tokv[:, 3, 0:NT], tokv[:, 1, 0:NT], tokv[:, 2, 0:NT], ADD))
                v.then(V.reciprocal(tokv[:, 3, 0:NT], tokv[:, 3, 0:NT]))
                for c in range(2):
                    v.then(tt(tokv[:, 1 + c, 0:NT], tokv[:, 1 + c, 0:NT], tokv[:, 3, 0:NT], MUL))
                for t in range(NT):
                    for c in range(2):
                        b = 2 * t + c
                        dve.wait_ge(S("row_hi"), b + 1)
                        tt(t_lo[:, t, c * 512:(c + 1) * 512], bank[b][:, :], t_hi[:, t, c * 512:(c + 1) * 512].bitcast(f32), SUB).then_inc(S("row_lo"), 1)
                dve.wait_ge(S("places"), 1)
                counts = bank[1][:, 0:NE]
                v.then(ts(chunks[:, :], counts, float(P), 1.0, ALU.is_gt, ADD))
                for c in range(2, TOK // P):
                    v.then(stt(chunks[:, :], counts, float(c * P), chunks[:, :], ALU.is_gt, ADD))
                v.then(V.memset(ends[:, :, :], 0.0))
                v.then(V.tensor_copy(ends[:, 0, 8:], chunks[:, :]))
                for i in range(4):
                    src, dst = ends[:, i % 2, :], ends[:, (i + 1) % 2, :]
                    v.then(tt(dst[:, 8:], src[:, 8:], src[:, 8 - (1 << i):8 - (1 << i) + NE], ADD))
                end = ends[:, 0, 8:]
                v.then(tt(starts[:, :], end, chunks[:, :], SUB))
                it = iota[:, 0:NI].unsqueeze(2).to_broadcast([P, NI, NE])
                v.then(tt(before_end[:, :, :], it, end.unsqueeze(1).to_broadcast([P, NI, NE]), ALU.is_ge))
                v.then(V.reduce_sum(item_f[:, :], before_end[:, :, :], AX.X))
                v.then(V.tensor_copy(items_i[0:1, 0:NI], item_f[0:1, :]))
                ts(items_i[0:1, NI:NI + 1], end[0:1, NE - 1:NE], -1.0, None, ADD).then_inc(S("items_ok"), 1)
                st = starts[:, :].unsqueeze(1).to_broadcast([P, NT, NE])
                v.then(ts(e3(row(6)), st, float(P), None, MUL))
                v.then(tt(row(7), row(6), bank[0][:, 0:W], ADD))
                v.step(V.memset(posm[:, :, :], 0.0))
                v.then(ts(item_base[:, :], iota[:, 0:NI + 1], float(P), -1.0, MUL, ADD))
                ib = item_base[:, :].unsqueeze(1).to_broadcast([P, NT, NI + 1])
                rel = rt[:, 8:10, :].rearrange("p a n -> p (a n)")[:, 0:NT * (NI + 1)].rearrange("p (t i) -> p t i", t=NT)
                for c in range(2):
                    v.then(tt(row(6), row(7), row(3 + c), MUL))
                    v.then(V.reduce_sum(tokv[:, 4 + c, 0:NT], e3(row(6)), AX.X))
                    v.then(tt(rel, tokv[:, 4 + c, 0:NT].unsqueeze(2).to_broadcast([P, NT, NI + 1]), ib, SUB))
                    v.then(stt(rel, rel, float(P), rel, ALU.is_le, MUL))
                    v.then(stt(posm[:, 0:NT, :], rel, 0.0, posm[:, 0:NT, :], ALU.max, ADD))
                    v.then(ts(rowid[:, c:c + 2 * NT - 1:2], tokv[:, 4 + c, 0:NT], float(P), None, ADD))
                v.then(ts(posm[:, :, :], posm[:, :, :], -1.0, None, ADD))

                dve.wait_ge(S("lo"), NU)
                dve.wait_ge(S("zr"), total)
                dve.sem_inc(S("e_lo"), EW)
                def esplit(i, j):
                    dve.wait_ge(S("e_hi"), i * EW + j + 1 + EW)
                    dve.wait_ge(S("e_used"), i * EW + j + 1)
                    tt(half_unit(wlo, j % EP), estage(j), half_unit(whi, j % EP).bitcast(f32), SUB).then_inc(S("e_lo"), 1)

                def picks(i, col):
                    dve.wait_ge(S("g_lo"), i * 2 + 2)
                    for t in range(NT):
                        ins = ts(pick[:, t, :], iota[:, :], posm[:, t, col], None, ALU.is_equal)
                        if t < NT - 1:
                            ins.then_inc(S("pick_t"), 1)
                    ins.then_inc(S("pick"), 1)

                def gathered(i, c):
                    dve.wait_ge(S("g_lo"), i * 2 + c + 3)
                    dve.wait_ge(S("e_used"), i * EW - 4 + EP)
                    V.tensor_copy(xg_lo[:, 4 * c:4 * c + 4, :].rearrange("p k n -> p (k n)"), bank[4 + c][:, :]).then_inc(S("xg_lo"), 1)

                def item(i, more):
                    for j in range(6, EW):
                        esplit(i, j)
                    if more:
                        esplit(i + 1, 0)
                    dve.wait_ge(S("silu"), i + 1)
                    dve.wait_ge(S("e_used"), i * EW + 8 + EP)
                    tt(act_a[:, :], act_s[:, :], bank[1][:, :], MUL).then_inc(S("act_a"), 1)
                    if more:
                        gathered(i + 1, 0)
                    dve.wait_ge(S("a_hi"), i + 1)
                    tt(a_lo[:, :, :].rearrange("p k n -> p (k n)"), bank[0][:, :], a_hi[:, :, :].rearrange("p k n -> p (k n)").bitcast(f32), SUB).then_inc(S("a_lo"), 1)
                    if more:
                        gathered(i + 1, 1)
                        esplit(i + 1, 1)
                        picks(i + 2, bass.ds(i + 2, 1))
                        for j in range(2, 6):
                            esplit(i + 1, j)

                for j in range(6):
                    esplit(0, j)
                dve.wait_ge(S("items_ok"), 1)
                last = dve.value_load(items_i[0:1, NI:NI + 1], min_val=NE - 1, max_val=NI - 1)
                picks(0, slice(0, 1))
                picks(1, slice(1, 2))
                gathered(0, 0)
                gathered(0, 1)
                with dve.Fori(0, last) as i:
                    item(i, True)
                item(last, False)
                dve.wait_ge(S("y_out"), (last + 3) * 16)
                dve.sem_inc(S("rows_ok"), 1)
                for t in range(NT):
                    for c in range(2):
                        dve.wait_ge(S(f"yg{c}"), (t + 1) * 16)
                    if t >= 2:
                        dve.wait_ge(S("combT"), t - 1)
                    ts(comb[:, t % 2, :], yg[:, 0, :], tokv[:, 1, t:t + 1], None, MUL).then_inc(S("comb0"), 1)
                    dve.wait_ge(S("comb0"), t + 1)
                    stt(comb[:, t % 2, :], yg[:, 1, :], tokv[:, 2, t:t + 1], comb[:, t % 2, :], MUL, ADD).then_inc(S("combined"), 1)
                    dve.wait_ge(S("combT"), t + 1)
                    for k in range(KT):
                        b = 2 * (t % 2) + k // 4
                        s = t // 2
                        c_ = slice(t * P, (t + 1) * P)
                        stt(xT[:, k, c_], bank[b][:, (k % 4) * P:(k % 4 + 1) * P], shift(5, k, s), xT[:, k, c_], MUL, ADD).then_inc(S("x_moe"), 1)
                dve.wait_ge(S("x_moe"), NT * KT)
                dve.sem_inc(S("moe_x"), 1)
                if l < DEPTH - 1:
                    dve.wait_ge(sem("all", "engine_done"), 4 * (l + 1))
                    dve.sem_clear(range(numbers[0], numbers[-1] + 1)).then_inc(sem("all", "layer_done"), 1)
                else:
                    for t in range(2):
                        for c in range(2):
                            dve.wait_ge(sem("all", "oT"), 2 * t + c + 1)
                            V.tensor_copy(orow[:, t, c * 512:(c + 1) * 512], bank[2 * t + c][:, :]).then_inc(sem("all", "orow_ok"), 1)
                    dve.sem_inc(sem("all", "layer_done"), 1)

        @block.tensor
        def _(pe):
            MM = nc.tensor.matmul

            def T_(o, i, n=P):
                return nc.tensor.transpose(o, i, ident[0:n, 0:n])

            pe.wait_ge(sem("all", "const_in"), 11 * 16)
            for l in range(DEPTH):
                T = span(l)
                NS = seqs(l)
                NF = 3 if NS == 2 else 2
                NT = T // P
                S = lambda name, l=l: sem(l, name)
                if l > 0:
                    pe.wait_ge(sem("all", "layer_done"), l)
                    pe.sem_inc(sem("all", "layer_begun"), 1)
                pe.wait_ge(S("vec_in"), 16 * 16)
                T_(bank[0][:, 0:NVEC1], vrow1[0:NVEC1, :], NVEC1)
                T_(bank[0][:, NVEC1:NVEC1 + NVEC2], vrow2[0:NVEC2, :], NVEC2).then_inc(S("vecT"), 1)
                if l == 0:
                    pe.wait_ge(sem("all", "c_silu"), 1)
                    T_(bank[1][:, 0:16], crow_s[:, :], 16).then_inc(sem("all", "cT"), 1)
                    pe.wait_ge(sem("all", "x_in"), 32)
                    for k in range(KT):
                        if k == 0:
                            pe.wait_ge(S("vec_ok"), 1)
                        if k == 1:
                            pe.wait_ge(sem("all", "c_lo"), 1)
                        for t in range(4):
                            ins = T_(bank[k][:, t * P:(t + 1) * P], xrow[:, t, k * P:(k + 1) * P])
                        ins.then_inc(sem("all", "xt"), 1)
                    pe.wait_ge(sem("all", "xt_act"), 4)
                    pe.wait_ge(sem("all", "xt_dve"), 4)
                for k in range(KT):
                    pe.wait_ge(S("n1_sq"), k + 1)
                    MM(bank[2][:, :], ones[:, :], sq[:, k % 2, :], start=(k == 0), stop=(k == KT - 1)).then_inc(S("n1_stat"), 1)

                def unit_ready(n):
                    pe.wait_ge(S("lo"), n + 1)

                def tile_free(m):
                    if m >= 2:
                        pe.wait_ge(S(f"zf{m % 2}"), m // 2)

                def three(o, w, x_, start, stop):
                    MM(o, w[0], x_[0], start=start, stop=False)
                    MM(o, w[0], x_[1], start=False, stop=False)
                    return MM(o, w[1], x_[0], start=False, stop=stop)

                def mod_columns(jj):
                    mm = first_tile[at["mod", jj]]
                    pe.wait_ge(S(f"zf{mm % 2}"), mm // 2 + 1)
                    for c in range(2):
                        col = (2 * jj + c) * 2
                        ins = MM(bank[7][:, col:col + 2], modrow[:, jj % 2, c * P:(c + 1) * P], fold[:, :], start=True, stop=True)
                    ins.then_inc(S("modcol"), 1)

                mods = 0
                for n, (kind, j) in enumerate(units):
                    m = first_tile[n]
                    unit_ready(n)
                    hi, lo = unit_view(whi[n % RING], n), unit_view(wlo[n % RING], n)
                    if kind == "mod":
                        tile_free(m)
                        if n == 0 and l == 0:
                            pe.wait_ge(sem("all", "c_lo"), 1)
                        for k in range(KT):
                            MM(bank[m % 2][:, 0:UW], cst[:, k, :], hi[:, k, :], start=(k == 0), stop=False)
                            ins = MM(bank[m % 2][:, 0:UW], cst[:, k, :], lo[:, k, :], start=False, stop=(k == KT - 1))
                        ins.then_inc(S("zr"), 1)
                    if kind in ("in", "gate", "out"):
                        if kind == "in" and j == 2:
                            N = TOK
                        else:
                            N = T
                        xh, xl = (m_hi, m_lo) if kind == "out" else (h_hi, h_lo)
                        for t in range(2):
                            tile_free(m + t)
                            for k in range(KT):
                                if n == at["in", 0] and t == 0:
                                    pe.wait_ge(S("h_lo"), k + 1)
                                if n == at["out", 0] and t == 0:
                                    pe.wait_ge(S("m_lo"), k + 1)
                                c = slice(t * P, (t + 1) * P)
                                ins = three(bank[(m + t) % 2][:, 0:N], (hi[:, k, c], lo[:, k, c]), (xh[:, k, 0:N], xl[:, k, 0:N]), k == 0, k == KT - 1)
                            ins.then_inc(S("zr"), 1)
                    if kind in ("proj_h", "proj_a", "proj_c"):
                        xh, xl, nk = {"proj_h": (oh_hi, oh_lo, 2), "proj_a": (oa_hi, oa_lo, 4), "proj_c": (oc_hi, oc_lo, 2)}[kind]
                        name, cnt = {"proj_h": ("oh_lo", 2), "proj_a": ("oa_lo", 4), "proj_c": ("oc_lo", 2)}[kind]
                        pe.wait_ge(S(name), cnt)
                        for t in range(n_tiles[kind]):
                            tile_free(m + t)
                            c = slice(t * P, (t + 1) * P)
                            for k in range(nk):
                                ins = three(bank[(m + t) % 2][:, 0:T], (hi[:, k, c], lo[:, k, c]), (xh[:, k, 0:T], xl[:, k, 0:T]), k == 0, k == nk - 1)
                            ins.then_inc(S("zr"), 1)
                    upto = sum(1 for u in units[:n + 1] if u[0] == "mod")
                    if not (kind == "mod" and j not in (7, 23)):
                        target = upto
                    else:
                        target = upto - 1
                    while mods < target:
                        mod_columns(mods)
                        mods += 1
                    if n == 0:
                        pe.wait_ge(S("fil_in"), 16 * 5)
                        MM(bank[3][0:64, 0:SEQ], fw1[:, :], feat[:, :], start=True, stop=True).then_inc(S("f_mm"), 1)
                    if n == 1:
                        pe.wait_ge(S("f_sin"), 1)
                        MM(bank[3][0:64, 0:SEQ], fw2[:, :], fh[:, 0, :], start=True, stop=True).then_inc(S("f_mm"), 1)
                    if n == 2:
                        pe.wait_ge(S("f_sin"), 2)
                        for t in range(2):
                            MM(bank[4 + t][:, :], fh[:, 1, t * P:(t + 1) * P], fw3[:, :], start=True, stop=True).then_inc(S("f_mm"), 1)
                    if n == 3:
                        pe.wait_ge(S("f_abs"), 2)
                        for t in range(2):
                            ins = MM(bank[6][:, :], ones[:, :], habs[:, t, :], start=(t == 0), stop=(t == 1))
                        ins.then_inc(S("f_mm"), 1)
                    if n == 4:
                        pe.wait_ge(S("f_sd"), 1)
                        for f in range(2):
                            o = bank[3][:, f * SEQ:(f + 1) * SEQ]
                            for t in range(2):
                                MM(o, fwd0[:, 0, t, f * P:(f + 1) * P], hs[:, t, :], start=(t == 0), stop=False)
                            MM(o, ones[0:1, :], hrow_d[:, :], start=False, stop=True)
                        for f in range(2):
                            o = bank[4][:, f * SEQ:(f + 1) * SEQ]
                            for t in range(2):
                                ins = MM(o, fwd0[:, 1, t, f * P:(f + 1) * P], hd[:, t, :], start=(t == 0), stop=(t == 1))
                        ins.then_inc(S("f_mm"), 1)
                    if n == at["mod", 11]:
                        pe.wait_ge(S("q_sq"), 4)
                        for i in range(4):
                            for t in range(NT):
                                c = t * NH + 2 * i
                                ins = MM(bank[6][:, c:c + 2], zsq[:, i, t * P:(t + 1) * P], headsum[:, :], start=True, stop=True)
                        ins.then_inc(S("q_stat"), 1)
                        for i in range(4):
                            pe.wait_ge(S("q_g"), i + 1)
                            MM(bank[2 + i // 2][:, (i % 2) * SEQ:(i % 2 + 1) * SEQ], rot[:, :], q[:, i, 0:SEQ], start=True, stop=True).then_inc(S("q_rot"), 1)
                    if n == at["mod", 12]:
                        pe.wait_ge(S("k_sq"), 1)
                        pe.wait_ge(S("H_ok"), 1)
                        MM(bank[4][:, :], headmean[:, :], ksq[:, :], start=True, stop=True).then_inc(S("k_stat"), 1)
                        mv = first_tile[at["in", 2]] + 1
                        pe.wait_ge(S(f"zf{mv % 2}"), mv // 2 + 1)
                        for t in range(4):
                            ins = T_(bank[5][:, t * P:(t + 1) * P], vT[:, t * P:(t + 1) * P])
                        ins.then_inc(S("vrows"), 1)
                    if n == at["mod", 13]:
                        pe.wait_ge(S("k_g"), 1)
                        MM(bank[4][:, 0:SEQ], rot[:, :], kraw[:, 0:SEQ], start=True, stop=True).then_inc(S("k_rot"), 1)
                    if n == at["mod", 19]:
                        pe.wait_ge(S("v_ok"), 1)
                        pe.wait_ge(S("q_ok"), 4)
                        pe.wait_ge(S("u"), 2)
                        for b in range(2):
                            for s in range(NS):
                                for c in range(2):
                                    o = s * SEQ + c * P
                                    ins = T_(bank[5 + b][:, o:o + P], zhy[:, 2 + c, s * SEQ + b * P:s * SEQ + (b + 1) * P])
                            ins.then_inc(S("uT"), 1)
                    if n == at["in", 6]:
                        pe.wait_ge(S("tab_in"), 32)
                        pe.wait_ge(S("u_act"), 1)
                        pe.wait_ge(S("u_dve"), 1)
                        pe.wait_ge(S("k_ok"), 1)
                        for f in range(2):
                            for part in range(2):
                                for t in range(2):
                                    ins = MM(bank[2 + 2 * f + part][:, 0:T], fwd[:, part, t, f * P:(f + 1) * P], urow[:, t, 0:T], start=(t == 0), stop=(t == 1))
                                ins.then_inc(S("U"), 1)
                    if n == at["mod", 22]:
                        pe.wait_ge(S("Y"), 2 * NS)
                        for c in range(2):
                            for s in range(NS):
                                for f in range(2):
                                    for part in range(2):
                                        ins = MM(bank[5 + c][:, s * SEQ:(s + 1) * SEQ], Y[:, part, f, s * SEQ + c * P:s * SEQ + (c + 1) * P],
                                                 inv[:, part, f, :], start=(f + part == 0), stop=(f + part == 2))
                            ins.then_inc(S("y_hy"), 1)

                    i = n - HEAD0
                    if 1 <= i <= NH:
                        pe.wait_ge(S("probs"), NT * i)
                        pe.wait_ge(S("oh_lo"), 2)
                        if i >= 2:
                            pe.wait_ge(S("pT_act"), NS * (i - 1))
                            pe.wait_ge(S("pT_dve"), i - 1)
                        for half in range(2):
                            for kt in range(2):
                                for c in range(2):
                                    ins = T_(bank[5 + half][:, kt * 256 + c * P:kt * 256 + (c + 1) * P], probs[:, c, (2 * half + kt) * P:(2 * half + kt + 1) * P])
                            ins.then_inc(S("pT"), 1)
                    if 0 <= i < NH:
                        if i == 0:
                            pe.wait_ge(S("k_ok"), 1)
                            pe.wait_ge(S("q_ok"), 4)
                        else:
                            pe.wait_ge(S("exp"), NT * i)
                        b0 = 64 * (i % 2)
                        kk = kd[b0:b0 + 64, i // 4, :]
                        for c in range(NT):
                            qq = q[b0:b0 + 64, i // 2, c * P:(c + 1) * P]
                            if c < 2:
                                ins = MM(bank[2 + c][:, :], qq, kk, start=True, stop=True)
                            else:
                                ins = MM(bank[4][:, (c - 2) * 256:(c - 1) * 256], qq, kk[:, SEQ:TOK], start=True, stop=True)
                        ins.then_inc(S("score"), 1)
                    if 1 <= i <= NH:
                        if NS == 2:
                            pe.wait_ge(S("pT_act"), NS * (i - 1) + 1)
                            for kt in range(2):
                                for c in range(2):
                                    ins = T_(bank[5][:, kt * 256 + c * P:kt * 256 + (c + 1) * P], probs[:, 2, c * 256 + kt * P:c * 256 + (kt + 1) * P])
                            ins.then_inc(S("pT"), 1)
                        h = i - 1
                        if h % 2 == 0:
                            if h == 0:
                                pe.wait_ge(S("mod_done"), 1)
                            else:
                                pe.wait_ge(S("oa_lo"), h // 2)
                        vv = lambda kt: vr[:, kt, 64 * (h // 4):64 * (h // 4) + 64]
                        o = bank[7][64 * (h % 2):64 * (h % 2) + 64, :]
                        pe.wait_ge(S("pT_act"), NS * (i - 1) + 1)
                        pe.wait_ge(S("pT_dve"), i)
                        for kt in range(4):
                            ins = MM(o[:, 0:SEQ], vv(kt), pT[:, kt // 2, (kt % 2) * 256:(kt % 2 + 1) * 256], start=(kt == 0), stop=(kt == 3))
                        if NS == 2:
                            pe.wait_ge(S("pT_act"), NS * i)
                            for kt in range(2):
                                ins = MM(o[:, SEQ:TOK], vv(2 + kt), pT[:, 2, kt * 256:(kt + 1) * 256], start=(kt == 0), stop=(kt == 1))
                        ins.then_inc(S("pv"), 1)
                    if n == at["gate", 8]:
                        pe.wait_ge(S("conv_ok"), 1)
                        for t in range(2):
                            ins = MM(bank[5][:, 0:T], ones[:, :], conv[:, t, 0:T], start=(t == 0), stop=(t == 1))
                        ins.then_inc(S("cf_mean"), 1)
                    if n == at["gate", 9]:
                        pe.wait_ge(S("cf_sq"), 2)
                        for t in range(2):
                            ins = MM(bank[6][:, 0:T], ones[:, :], csq[:, t, 0:T], start=(t == 0), stop=(t == 1))
                        ins.then_inc(S("cf_var"), 1)

                for k in range(KT):
                    pe.wait_ge(S("n2_sq"), k + 1)
                    MM(bank[2][:, 0:T], ones[:, :], sq[:, k % 2, 0:T], start=(k == 0), stop=(k == KT - 1)).then_inc(S("n2_stat"), 1)
                pe.wait_ge(S("x_back"), 32)
                pe.wait_ge(S("h2"), KT)
                for t in range(NT):
                    for k in range(KT):
                        ins = MM(bank[0][:, t * NE:(t + 1) * NE], h2T[:, k, t * P:(t + 1) * P], wr[:, k, :], start=(k == 0), stop=(k == KT - 1))
                ins.then_inc(S("logits"), 1)
                pe.wait_ge(S("affin"), 1)
                for t in range(NT):
                    for c in range(2):
                        for k in range(4):
                            ins = T_(bank[2 * t + c][:, k * P:(k + 1) * P], h2T[:, 4 * c + k, t * P:(t + 1) * P])
                        ins.then_inc(S("rows"), 1)
                pe.wait_ge(S("routed"), 1)
                pe.wait_ge(S("row_lo"), 2)
                mk = lambda t: rt[:, 5, t * NE:(t + 1) * NE]
                for t in range(NT):
                    for t0 in range(t):
                        MM(bank[0][:, t * NE:(t + 1) * NE], ones[:, :], mk(t0), start=(t0 == 0), stop=False)
                    MM(bank[0][:, t * NE:(t + 1) * NE], before[:, :], mk(t), start=(t == 0), stop=True)
                for t in range(NT):
                    ins = MM(bank[1][:, 0:NE], ones[:, :], mk(t), start=(t == 0), stop=(t == NT - 1))
                ins.then_inc(S("places"), 1)
                pe.wait_ge(S("row_lo"), 2 * NT)

                pe.sem_inc(S("e_used"), EP)
                pe.sem_inc(S("g_lo"), 2)
                pe.wait_ge(S("items_ok"), 1)
                last = pe.value_load(items_i[0:1, NI:NI + 1], min_val=NE - 1, max_val=NI - 1)

                def gather(i, q0, q1):
                    for q_ in range(q0, q1):
                        part, kk = q_ // KT, q_ % KT
                        c, k = kk // 4, kk % 4
                        src, b0, name = (t_hi, 2, "g_hi") if part == 0 else (t_lo, 4, "g_lo")
                        if q_ == 0:
                            pe.wait_ge(S("pick"), i + 1)
                        for t in range(NT):
                            ins = MM(bank[b0 + c][:, k * P:(k + 1) * P], src[:, t, kk * P:(kk + 1) * P], pick[:, t, :], start=(t == 0), stop=(t == NT - 1))
                        if k == 3:
                            ins.then_inc(S(name), 1)

                GSTEPS = (0, 1, 2, 3, 5, 6, 8, 10, 13)

                def item(i, more):
                    pe.wait_ge(S("xg_hi"), i * 2 + 2)
                    pe.wait_ge(S("xg_lo"), i * 2 + 2)
                    for j in range(8):
                        pe.wait_ge(S("e_lo"), i * EW + j + 1 + EW)
                        hi = half_unit(whi, j % EP).rearrange("p (k n) -> p k n", k=2)
                        lo = half_unit(wlo, j % EP).rearrange("p (k n) -> p k n", k=2)
                        for k in range(2):
                            kk = 2 * (j % 4) + k
                            o = bank[j // 4][:, :]
                            MM(o, xg_hi[:, kk, :], hi[:, k, :], start=(kk == 0), stop=False)
                            MM(o, xg_hi[:, kk, :], lo[:, k, :], start=False, stop=False)
                            ins = MM(o, xg_lo[:, kk, :], hi[:, k, :], start=False, stop=(kk == KT - 1))
                        ins.then_inc(S("e_used"), 1)
                        if more:
                            gather(i + 1, GSTEPS[j], GSTEPS[j + 1])
                    pe.wait_ge(S("act_a"), i + 1)
                    for k in range(4):
                        ins = T_(bank[0][:, k * P:(k + 1) * P], act_a[:, k * P:(k + 1) * P])
                    ins.then_inc(S("aT"), 1)
                    if more:
                        gather(i + 1, 13, 16)
                    pe.wait_ge(S("a_hi"), i + 1)
                    pe.wait_ge(S("a_lo"), i + 1)
                    pe.wait_ge(S("e_yev"), i + 1)
                    for j in range(8, EW):
                        pe.wait_ge(S("e_lo"), i * EW + j + 1 + EW)
                        hi, lo = half_unit(whi, j % EP), half_unit(wlo, j % EP)
                        kk = j - 8
                        for c in range(2):
                            o = bank[6 + c][:, :]
                            cc = slice(c * 512, (c + 1) * 512)
                            MM(o, a_hi[:, kk, :], hi[:, cc], start=(kk == 0), stop=False)
                            MM(o, a_hi[:, kk, :], lo[:, cc], start=False, stop=False)
                            ins = MM(o, a_lo[:, kk, :], hi[:, cc], start=False, stop=(kk == 3))
                        ins.then_inc(S("e_used"), 1)

                gather(0, 0, 16)
                with pe.Fori(0, last) as i:
                    item(i, True)
                item(last, False)
                for t in range(NT):
                    pe.wait_ge(S("combined"), t + 1)
                    if t >= 2:
                        pe.wait_ge(S("x_moe"), (t - 1) * KT)
                    for k in range(KT):
                        b = 2 * (t % 2) + k // 4
                        ins = T_(bank[b][:, (k % 4) * P:(k % 4 + 1) * P], comb[:, t % 2, k * P:(k + 1) * P])
                    ins.then_inc(S("combT"), 1)
                pe.sem_inc(sem("all", "engine_done"), 1)
                if l == DEPTH - 1:
                    pe.wait_ge(S("moe_x"), 1)
                    for t in range(2):
                        for c in range(2):
                            for k in range(4):
                                ins = T_(bank[2 * t + c][:, k * P:(k + 1) * P], xT[:, 4 * c + k, t * P:(t + 1) * P])
                            ins.then_inc(sem("all", "oT"), 1)


_INS = ["x", "c", "ctx", "c_ctx", "w_mod", "b_mod", "g_norm1", "g_norm2", "w_in", "q_norm", "k_norm",
        "hy_short_w", "hy_short_b", "hy_w1", "hy_b1", "hy_w2", "hy_b2", "hy_w3", "hy_freq", "hy_bias",
        "cf_dw_w", "cf_dw_b", "cf_ln_g", "cf_ln_b", "p_attn", "p_hyena", "p_conv", "w_out",
        "w_router", "b_router", "w_exp_gate", "w_exp_up", "w_exp_down"]


def kernel(**inputs):
    import numpy as _np
    import concourse.bacc as _bacc
    from concourse import mybir as _mybir
    from concourse.bass_utils import run_bass_kernel_spmd as _run

    nc = _bacc.Bacc("TRN2", target_bir_lowering=False, num_devices=1)
    consts, f32 = shape_constants(inputs["x"].shape[1], inputs["x"].shape[2] // 4)
    arrays, aps = {}, {}
    for name in _INS:
        arrays[f"in_{name}"] = _np.ascontiguousarray(inputs[name])
    for name, a in consts.items():
        arrays[f"in_{name}"] = _np.ascontiguousarray(_np.asarray(a, dtype=f32))
    for name, a in arrays.items():
        aps[name[3:]] = nc.dram_tensor(name, a.shape, _mybir.dt.from_np(a.dtype), kind="ExternalInput").ap()
    out = nc.dram_tensor("out_0", inputs["x"].shape, _mybir.dt.float32, kind="ExternalOutput").ap()
    hybrid_backbone(nc, aps, out)
    r = _run(nc, [arrays], core_ids=[0])
    return r.results[0]["out_0"]
```

```python
import math
from contextlib import ExitStack

import numpy as np
import concourse.bass as bass
from concourse import mybir


def shape_constants(seq, hyena_w):
    f = np.float32
    half, quarter = 32, 16
    t = np.arange(seq)
    inv = 10000.0 ** (-np.arange(0, half, 2) / half)
    row, col = (t // 64)[:, None] * inv, (t % 64)[:, None] * inv
    ang = np.concatenate([row, row, col, col], axis=-1).T
    cos, sin = np.cos(ang), np.sin(ang)
    rot = np.zeros((64, 64))
    for b in range(2):
        for i in range(quarter):
            rot[b * half + i, b * half + quarter + i] = -1.0
            rot[b * half + quarter + i, b * half + i] = 1.0
    rot2 = np.kron(np.eye(2), rot)
    theta = 2.0 * np.pi * (np.arange(seq) + 0.5) / (2 * seq)
    cc, ss = np.cos(np.outer(t, theta)), np.sin(np.outer(t, theta))
    tl = np.linspace(0.0, 1.0, seq)[:, None]
    w = 2.0 * np.pi * np.arange(seq)[:, None] / seq
    fr = np.linspace(1e-4, 15, 16)[None, :]
    feat = np.concatenate([tl, np.cos(fr * w), -np.sin(fr * w)], axis=-1)
    lo, hi = math.log(1e-2) / 1.5, math.log(1e-2) / 0.3
    deltas = np.tile(np.linspace(lo, hi, hyena_w), 2)
    decay = np.exp(-tl * np.abs(deltas))
    tile2 = lambda a: np.ascontiguousarray(a.reshape(2, 128, -1).transpose(1, 0, 2)).reshape(128, -1)
    i = np.arange(128)
    return {
        "c_ident": np.eye(128), "c_ones": np.ones((128, 128)),
        "c_headmean": np.kron(np.eye(2), np.ones((64, 64))) / 64.0,
        "c_before": (i[:, None] < i[None, :]), "c_iota": np.broadcast_to(i[None, :], (128, 128)),
        "c_rot": rot2.T, "c_headsum": np.kron(np.eye(2), np.ones((64, 1))),
        "c_fold": np.concatenate([np.eye(2), np.eye(2)]),
        "c_cos": np.concatenate([cos, cos]), "c_sin": np.concatenate([sin, sin]),
        "c_fwd": np.concatenate([tile2(cc), tile2(ss)], axis=1),
        "c_inv": np.concatenate([tile2(cc.T / seq), tile2(ss.T / seq)], axis=1),
        "c_feat": feat.T, "c_decay": tile2(decay),
        "c_first": np.broadcast_to(np.concatenate([16.0 - np.arange(16), 4.0 - np.arange(4), 1.0 + np.arange(16)])[None, :], (128, 36)),
    }, f


def hybrid_backbone(nc, A, out):
    f32, f32r, i32 = mybir.dt.float32, mybir.dt.float32r, mybir.dt.int32
    ALU, ACT, AX = mybir.AluOpType, mybir.ActivationFunctionType, mybir.AxisListType
    MUL, ADD, SUB = ALU.mult, ALU.add, ALU.subtract

    P = 128
    SEQ, D = A["x"].shape[1], A["x"].shape[2]
    DEPTH, NE, FF = A["w_mod"].shape[0], A["w_exp_gate"].shape[1], A["w_exp_gate"].shape[3]
    KT = D // P
    TOK = 2 * SEQ
    EPS = 1e-6
    UW = 256
    UE = KT * UW
    RING = 3
    BIG = 1.0e30
    NI = NE + (2 * TOK - 1) // P
    TWO_PI_HI, TWO_PI_LO, ROUND = 6.28125, 2 * math.pi - 6.28125, 1.5 * 2.0 ** 23
    PI = 3.1415925

    LAYER_SEMS = (
        "hn", "mean_sq", "root",
        "H_ok", "U", "Y", "aT", "a_hi", "a_lo", "act_a", "affin", "cf_mean", "cf_n", "cf_o",
        "cf_sq", "cf_var", "cf_xc", "combT", "lg", "lgT", "combined", "conv_ok", "e_hi", "e_lo",
        "e_used", "e_yev", "ew0", "ew1", "ew2", "ew3", "ew4", "ew5", "ew6", "ew7", "ew8", "ew9", "ew10", "ew11",
        "exp", "f_abs", "f_arg", "f_mm", "f_raw", "f_sd", "f_sin",
        "g_cols", "g_rows", "glu_free", "glu_ok", "h2", "h_hi", "h_lo", "hi",
        "hm", "hy_o", "k_g", "k_ok", "k_rot", "k_sq", "k_stat", "lo", "logits", "m_hi",
        "m_lo", "mg_a", "mg_c", "mg_h", "mod_done", "modcol", "moe_x", "n1_sq", "n1_stat", "n2_sq", "n2_stat", "nmax", "oa_hi", "oa_lo", "oc_hi", "oc_lo",
        "oh_hi", "oh_lo", "pT", "pT_act", "pT_dve", "pick", "places", "probs", "pv", "q_g", "q_ok", "q_rot", "q_sq", "q_stat", "items_ok", "routed", 
        "row_hi", "row_lo", "rows", "rows_ok", "score", "short", "silu", "tab_in", "u", "uT",
        "u_act", "u_dve", "v_ok", "vecT", "vec_ok", "vec_zero", "vrows", 
        "x_moe", "xg_hi", "xg_lo", "xr_a", "xr_d", "y_hy", "y_out", "zf0", "zf1",
        "zr", "vec_in", "fil_in", "fil2_in", "spill",
    )

    units = [("mod", j) for j in range(16)]
    for j in range(8):
        units += [("in", j), ("mod", 16 + j)]
    FIRST_GATE = len(units)
    units += [("gate", 4 + j) for j in range(4)] + [("proj_h", 0)]
    units += [("gate", j) for j in range(4)] + [("proj_a", 0), ("proj_a", 1)]
    units += [("gate", 8 + j) for j in range(4)] + [("proj_c", 0)]
    units += [("out", j) for j in range(4)]
    NU = len(units)
    at = {u: n for n, u in enumerate(units)}
    n_tiles = {"mod": 1, "in": 2, "gate": 2, "proj_h": 8, "proj_a": 4, "proj_c": 8, "out": 2}
    first_tile, total = [], 0
    for kind, _ in units:
        first_tile.append(total)
        total += n_tiles[kind]

    def unit_source(l, n):
        kind, j = units[n]
        if kind == "mod":
            return A["w_mod"][l, :, j * UW:(j + 1) * UW].rearrange("(k p) n -> p k n", p=P)
        if kind in ("in", "gate"):
            c = (j if kind == "in" else 8 + j) * UW
            return A["w_in"][l, :, c:c + UW].rearrange("(k p) n -> p k n", p=P)
        if kind == "proj_h":
            return A["p_hyena"][l].rearrange("(k p) n -> p k n", p=P)
        if kind == "proj_c":
            return A["p_conv"][l].rearrange("(k p) n -> p k n", p=P)
        if kind == "proj_a":
            return A["p_attn"][l, :, j * 512:(j + 1) * 512].rearrange("(k p) n -> p k n", p=P)
        return A["w_out"][l, :, j * UW:(j + 1) * UW].rearrange("(k p) n -> p k n", p=P)

    def unit_view(buf, n):
        k = {"proj_h": 2, "proj_c": 2, "proj_a": 4}.get(units[n][0], KT)
        return buf[:, :].rearrange("p (k n) -> p k n", k=k)

    HEAD0 = FIRST_GATE - 1
    NH = 8
    H_SLOT = at["mod", 8]
    Q_SLOT, K_SLOT, KROT_SLOT = at["mod", 17], at["mod", 18], at["in", 4]
    U_SLOT, Y_SLOT = at["mod", 21], at["in", 7]

    ctx = ExitStack()
    with ctx:
        base = [-(-nc.sbuf_base // 64) * 64]
        LIMIT = nc.sbuf_usable_end

        def at_byte(name, shape, dt, off):
            size = 4 * int(np.prod(shape[1:]))
            assert off + size <= LIMIT, (name, off + size - LIMIT)
            return nc.alloc_sbuf_tensor_at(name, shape, dt, offset=off)

        def keep(name, shape, dt=f32):
            off = base[0]
            base[0] += -(-4 * int(np.prod(shape[1:])) // 32) * 32
            return at_byte(name, shape, dt, off)

        def region(kib):
            off = base[0]
            base[0] += int(kib * 1024)
            assert base[0] <= LIMIT, (base[0] - LIMIT)
            return off

        stage = [keep(f"stage{i}", [P, UE]) for i in range(RING)]
        whi = [keep(f"whi{i}", [P, UE], f32r) for i in range(RING)]
        wlo = [keep(f"wlo{i}", [P, UE], f32r) for i in range(RING)]
        ident, ones = keep("ident", [P, P]), keep("ones", [P, P])
        headmean, before = keep("headmean", [P, P]), keep("before", [P, P])
        iota, rot = keep("iota", [P, P]), keep("rot", [P, P])
        headsum, fold, first = keep("headsum", [P, 2]), keep("fold", [4, 2]), keep("first", [P, 36])
        cosT, sinT = keep("cosT", [P, SEQ]), keep("sinT", [P, SEQ])
        cst = keep("cst", [P, KT, P], f32r)
        NVEC1, NVEC2 = 99, 62
        vec = keep("vec", [P, NVEC1 + NVEC2])
        modT = keep("modT", [P, 96])
        amp = keep("amp", [P, 2, KT, 2])
        modrow = keep("modrow", [4, 2, UW])
        rsq = keep("rsq", [P, 4, NH])
        small = keep("small", [P, 32])
        router_b = keep("router_b", [P, NE])
        glu = keep("glu", [P, 2, 2, SEQ + 30])
        CONV = region(4)
        conv = at_byte("conv", [P, 2, TOK], f32, CONV)
        R1, R2, R3, R4 = region(16), region(16), region(16), region(16)
        R5, R6, R7, R8 = region(8), region(8), region(8), region(8)
        R9, RK, RV = region(12), region(4), region(2)
        K = 1024
        xT = at_byte("xT", [P, KT, TOK], f32, R7)
        h_hi, h_lo = at_byte("h_hi", [P, KT, TOK], f32r, R1), at_byte("h_lo", [P, KT, TOK], f32r, R2)
        m_hi, m_lo = at_byte("m_hi", [P, KT, TOK], f32r, R1), at_byte("m_lo", [P, KT, TOK], f32r, R2)
        gates = at_byte("gates", [P, KT, TOK], f32, R3)
        merged = at_byte("merged", [P, KT, TOK], f32, R4)
        xrow = at_byte("xrow", [P, 4, D], f32, R4)
        vrow1, vrow2 = at_byte("vrow1", [P, P], f32, R5), at_byte("vrow2", [P, P], f32, R5 + 512)
        crow = at_byte("crow", [16, P], f32, R5 + 1024)
        crow_s = at_byte("crow_s", [16, P], f32, R5 + 1536)
        sq = at_byte("sq", [P, 2, TOK], f32, R5 + 2 * K)
        sq1 = at_byte("sq1", [P, KT, TOK], f32, R2)
        rs = at_byte("rs", [P, TOK], f32, R5 + 6 * K)
        hn = at_byte("hn", [P, 2, TOK], f32, R6)
        hm = at_byte("hm", [P, 2, TOK], f32, R6 + 4 * K)
        feat = at_byte("feat", [33, SEQ], f32, CONV)
        fw1, fw2 = at_byte("fw1", [33, 64], f32, CONV + K), at_byte("fw2", [64, 64], f32, CONV + K + 256)
        fh = at_byte("fh", [64, 2, SEQ], f32, CONV + 2 * K)
        fw3 = at_byte("fw3", [64, 512], f32, RV)
        hfil = at_byte("hfil", [P, 2, 512], f32, R9 + 4 * K)
        habs = at_byte("habs", [P, 2, 512], f32, R9 + 8 * K)
        hrow_d = at_byte("hrow_d", [1, SEQ], f32, R9 + 3 * K)
        decay = at_byte("decay", [P, 2, 512], f32, R4)
        fwd0 = at_byte("fwd0", [P, 2, 2, SEQ], f32, R4 + 4 * K)
        hinv = at_byte("hinv", [P, 512], f32, R4 + 8 * K)
        hs = at_byte("hs", [P, 2, SEQ], f32, R4 + 10 * K)
        hd = at_byte("hd", [P, 2, SEQ], f32, R4 + 12 * K)
        H = at_byte("H", [P, 2, 2, SEQ], f32, R9)
        zraw = at_byte("zraw", [P, 4, TOK], f32, R3)
        zsq = at_byte("zsq", [P, 4, TOK], f32, R3 + 8 * K)
        q = at_byte("q", [P, 4, TOK], f32, R5)
        kraw = at_byte("kraw", [P, TOK], f32, R6)
        ksq = at_byte("ksq", [P, TOK], f32, R6 + 2 * K)
        vT = at_byte("vT", [P, TOK], f32, R6 + 4 * K)
        krs = at_byte("krs", [P, TOK], f32, R6 + 6 * K)
        kd = at_byte("kd", [P, 2, TOK], f32, RK)
        vr = at_byte("vr", [P, 4, P], f32, RV)
        ropet = at_byte("ropet", [P, 2, SEQ], f32, R9 + 4 * K)
        zhy = at_byte("zhy", [P, 6, TOK], f32, R4)
        urow = at_byte("urow", [P, 2, TOK], f32, R7)
        fwd = at_byte("fwd", [P, 2, 2, SEQ], f32, R8)
        inv = at_byte("inv", [P, 2, 2, SEQ], f32, R8 + 4 * K)
        ytmp = at_byte("ytmp", [P, 2, TOK], f32, R3 + 8 * K)
        Y = at_byte("Y", [P, 2, 2, TOK], f32, R6)
        hyo = at_byte("hyo", [P, 2, TOK], f32, R3 + 8 * K)
        oh_hi, oh_lo = at_byte("oh_hi", [P, 2, TOK], f32r, R7), at_byte("oh_lo", [P, 2, TOK], f32r, R7 + 4 * K)
        gsig = at_byte("gsig", [P, 2, TOK], f32, R3 + 12 * K)
        probs = at_byte("probs", [P, 3, 512], f32, R9)
        pT = at_byte("pT", [P, 3, 512], f32, R9 + 6 * K)
        oa_hi, oa_lo = at_byte("oa_hi", [P, 4, TOK], f32r, R5), at_byte("oa_lo", [P, 4, TOK], f32r, R6)
        csq = at_byte("csq", [P, 2, TOK], f32, R9)
        crs = at_byte("crs", [P, TOK], f32, R9 + 4 * K)
        co = at_byte("co", [P, 2, TOK], f32, R9 + 6 * K)
        oc_hi, oc_lo = at_byte("oc_hi", [P, 2, TOK], f32r, R8), at_byte("oc_lo", [P, 2, TOK], f32r, R8 + 4 * K)
        t_hi, t_lo = at_byte("t_hi", [P, 4, D], f32r, R1), at_byte("t_lo", [P, 4, D], f32r, R2)
        h2T = at_byte("h2T", [P, KT, TOK], f32, R3)
        wr = at_byte("wr", [P, KT, NE], f32, R9)
        rt = at_byte("rt", [P, 14, 64], f32, R9 + 512)
        grp = at_byte("grp", [P, 8, 16], f32, R9 + 512 + 3584)
        posm = at_byte("posm", [P, 4, NI + 1], f32, R9 + 5 * K)
        tokv = at_byte("tokv", [P, 6, 4], f32, R9 + 5 * K + 512)
        rowid = at_byte("rowid", [P, 8], i32, R9 + 6 * K)
        chunks, starts = at_byte("chunks", [P, NE], f32, R9 + 6 * K + 64), at_byte("starts", [P, NE], f32, R9 + 6 * K + 128)
        ends = at_byte("ends", [P, 2, 8 + NE], f32, R9 + 6 * K + 192)
        item_base = at_byte("item_base", [P, NI + 1], f32, R9 + 6 * K + 384)
        item_f = at_byte("item_f", [P, NI], f32, R9 + 6 * K + 512)
        items_i = at_byte("items_i", [1, NI + 1], i32, R9 + 6 * K + 640)
        before_end = at_byte("before_end", [P, NI, NE], f32, R9 + 7 * K)
        xpick = at_byte("xpick", [P, D], f32, RK)
        zero_rows = at_byte("zero_rows", [P, D], f32, RK)
        xg_hi, xg_lo = at_byte("xg_hi", [P, KT, P], f32r, R4), at_byte("xg_lo", [P, KT, P], f32r, R4 + 4 * K)
        pick = at_byte("pick", [P, 4, P], f32r, R4 + 8 * K)
        act_s = at_byte("act_s", [P, FF], f32, R4 + 10 * K)
        act_a = at_byte("act_a", [P, FF], f32, R4 + 12 * K)
        a_hi, a_lo = at_byte("a_hi", [P, 4, P], f32r, R5), at_byte("a_lo", [P, 4, P], f32r, R5 + 2 * K)
        yrow = at_byte("yrow", [P, D], f32, R6 + 4 * K)
        HU, EW, EP = UE // 2, 12, 6
        stage_b = at_byte("stage_b", [P, 4 * HU], f32, R3)
        stage_c = at_byte("stage_c", [P, 2 * HU], f32, R5 + 4 * K)

        def half_unit(bufs, s):
            return bufs[s // 2][:, (s % 2) * HU:(s % 2 + 1) * HU]

        def estage(j):
            if j < 6:
                return half_unit(stage, j)
            return stage_b[:, (j - 6) * HU:(j - 5) * HU] if j < 10 else stage_c[:, (j - 10) * HU:(j - 9) * HU]

        yg = at_byte("yg", [P, 4, 2, D], f32, R1)
        mask_sums = at_byte("mask_sums", [P, 5 * NE], f32, R9 + 11 * K)
        lgT = at_byte("lgT", [NE, TOK], f32, R9 + 9 * K)
        comb = at_byte("comb", [P, 2, D], f32, R3 + 8 * K)
        orow = at_byte("orow", [P, 2, D], f32, R4)

        bank = [ctx.enter_context(nc.psum_tensor(f"bank{i}", [P, 512], f32)) for i in range(8)]

        x_spill = nc.dram_tensor("x_spill", (P, KT * TOK), f32, kind="Internal").ap()
        y_rows = nc.dram_tensor("y_rows", ((NI + 1) * P, D), f32, kind="Internal").ap()

        def row_bank(b):
            return bank[b % 7]

        sems = {name: ctx.enter_context(nc.semaphore(name)) for name in LAYER_SEMS}
        numbers = sorted(x.num for x in sems.values())
        assert numbers == list(range(numbers[0], numbers[0] + len(numbers)))

        def sem(l, name):
            if name in LAYER_SEMS:
                return sems[name]
            if (l, name) not in sems:
                sems[l, name] = ctx.enter_context(nc.semaphore(f"{name}_{l}"))
            return sems[l, name]

        class Program:

            def __init__(self, eng, name):
                self.eng, self.steps, self.count = eng, sem("all", name), 0

            def step(self, ins):
                self.count += 1
                ins.then_inc(self.steps, 1)

            def sync(self):
                self.eng.wait_ge(self.steps, self.count)

            def then(self, ins):
                self.step(ins)
                self.sync()

        block = ctx.enter_context(nc.Block())

        def span(l):
            return TOK if l < DEPTH - 1 else SEQ

        def seqs(l):
            return span(l) // SEQ

        def small_loads(eng, l):
            def load(l, name, dst, src):
                eng.dma_start(dst, src).then_inc(sem(l, name), 16)

            eng.wait_ge(sem(l, "vec_zero"), 1)
            rows = [(0, A["b_mod"][l].rearrange("(r p) -> r p", p=P)), (48, A["g_norm1"][l].rearrange("(r p) -> r p", p=P)),
                    (56, A["g_norm2"][l].rearrange("(r p) -> r p", p=P)),
                    (64, A["hy_short_w"][l].rearrange("k (c p) -> (k c) p", p=P)),
                    (82, A["hy_short_b"][l].rearrange("(r p) -> r p", p=P)), (88, A["cf_dw_b"][l].rearrange("(r p) -> r p", p=P)),
                    (90, A["cf_ln_g"][l].rearrange("(r p) -> r p", p=P)), (92, A["cf_ln_b"][l].rearrange("(r p) -> r p", p=P))]
            for r0, src in rows:
                load(l, "vec_in", vrow1[r0:r0 + src.shape[0], :], src)
            for r0, name in ((94, "q_norm"), (95, "k_norm")):
                for h in range(2):
                    load(l, "vec_in", vrow1[r0:r0 + 1, 64 * h:64 * h + 64], A[name][l:l + 1, :])
            for r0, name in ((96, "hy_b1"), (97, "hy_b2"), (98, "hy_freq")):
                load(l, "vec_in", vrow1[r0:r0 + 1, 0:64], A[name][l:l + 1, :])
            load(l, "vec_in", vrow2[0:NVEC2, :], A["cf_dw_w"][l].rearrange("k (c p) -> (k c) p", p=P))
            if l == 0:
                load("all", "c_in", crow[0:8, :], A["c"].rearrange("a (r p) -> (a r) p", p=P))
                load("all", "c_in", crow[8:16, :], A["c_ctx"].rearrange("(r p) -> r p", p=P))
                load("all", "c_in", router_b[:, :], A["b_router"].rearrange("(a n) -> a n", a=1).to_broadcast([P, NE]))
            load(l, "fil_in", feat[:, :], A["c_feat"])
            load(l, "fil_in", fw1[:, :], A["hy_w1"][l])
            load(l, "fil_in", fw2[:, :], A["hy_w2"][l])
            load(l, "fil_in", fw3[:, :], A["hy_w3"][l])
            load(l, "fil_in", hrow_d[:, :], A["hy_bias"][l:l + 1, :])

        @block.sync
        def _(sp):
            def load(l, name, dst, src):
                sp.dma_start(dst, src).then_inc(sem(l, name), 16)

            for name, t in (("c_ident", ident), ("c_ones", ones), ("c_headmean", headmean), ("c_before", before),
                            ("c_iota", iota), ("c_rot", rot), ("c_headsum", headsum), ("c_fold", fold),
                            ("c_first", first), ("c_cos", cosT), ("c_sin", sinT)):
                load("all", "const_in", t[:, :], A[name])
            for l in range(DEPTH):
                def unit(l, n):
                    if n >= RING:
                        sp.wait_ge(sem(l, "hi"), n - RING + 1)
                        sp.wait_ge(sem(l, "lo"), n - RING + 1)
                    sp.dma_start(unit_view(stage[n % RING], n), unit_source(l, n)).then_inc(sem("all", f"w{n % RING}"), 16)

                T = span(l)
                S = lambda name, l=l: sem(l, name)
                if l > 0:
                    sp.wait_ge(sem("all", "layer_done"), l)
                    sp.sem_inc(sem("all", "passed"), 1)
                    small_loads(sp, l)
                for n in range(NU):
                    if l == 0 or n >= RING:
                        unit(l, n)
                    if n == RING - 1:
                        if l == 0:
                            sp.wait_ge(sem("all", "xt_act"), 4)
                            sp.wait_ge(sem("all", "xt_dve"), 4)
                        load(l, "fil2_in", decay[:, :, :], A["c_decay"])
                        load(l, "fil2_in", fwd0[:, :, :, :], A["c_fwd"])
                    if n == 6:
                        load(l, "spill", x_spill, xT[:, :, :].rearrange("p k n -> p (k n)"))
                    if l == 0 and n == at["in", 1]:
                        sp.wait_ge(sem("all", "zeros"), 1)
                        for b in range(NE + 1, NI + 1):
                            load("all", "y_zeroed", y_rows[b * P:(b + 1) * P, :], zero_rows[:, :])
                    if n == at["in", 3]:
                        sp.wait_ge(sem(l, "spill"), 16)
                        sp.wait_ge(sem(l, "h_lo"), KT)
                        load(l, "tab_in", fwd[:, :, :, :], A["c_fwd"])
                        load(l, "tab_in", inv[:, :, :, :], A["c_inv"])
                sp.wait_ge(sem(l, "lo"), NU)

                def expert_unit(e, i, j):
                    sp.wait_ge(S("e_lo"), i * EW + j + 1)
                    if j == 8:
                        sp.sem_inc(sem("all", "passed"), 1)
                    w, r0, nr = ((A["w_exp_gate"], j % 4, 2 * P) if j < 4 else (A["w_exp_up"], j % 4, 2 * P) if j < 8
                                 else (A["w_exp_down"], j % 4, P))
                    src = w[l, bass.ds(e, 1), r0 * nr:(r0 + 1) * nr, :].rearrange("a (k p) n -> p (a k) n", p=P)
                    sp.dma_start(estage(j).rearrange("p (k n) -> p k n", k=nr // P), src).then_inc(S(f"ew{j}"), 16)

                def y_out(i):
                    sp.wait_ge(S("e_yev"), i + 1)
                    sp.dma_start(y_rows[bass.ds(i * P, P), :], yrow[:, :]).then_inc(S("y_out"), 16)

                def second_half(e, i):
                    for j in range(6, 10):
                        expert_unit(e, i, j)
                    y_out(i)
                    for j in range(10, EW):
                        expert_unit(e, i, j)

                for j in range(6):
                    expert_unit(0, 0, j)
                sp.wait_ge(S("rows"), 2 * (T // P))
                sp.wait_ge(S("items_ok"), 1)
                last = sp.value_load(items_i[0:1, NI:NI + 1], min_val=NE - 1, max_val=NI - 1)
                with sp.Fori(0, last) as i:
                    e = sp.value_load(items_i[0:1, bass.ds(i, 1)], min_val=0, max_val=NE - 1)
                    e_next = sp.value_load(items_i[0:1, bass.ds(i + 1, 1)], min_val=0, max_val=NE - 1)
                    second_half(e, i)
                    for j in range(6):
                        expert_unit(e_next, i + 1, j)
                second_half(NE - 1, last)
                y_out(last + 1)
                if l < DEPTH - 1:
                    sp.wait_ge(S("e_lo"), last * EW + 2 * EW)
                    for n in range(RING):
                        unit(l + 1, n)
                sp.sem_inc(sem("all", "engine_done"), 1)
                sp.wait_ge(sem("all", "layer_done"), l + 1)
            sp.wait_ge(sem("all", "rows_out"), 2 * 16)

        @block.gpsimd
        def _(pool):
            def load(l, name, dst, src):
                pool.dma_start(dst, src).then_inc(sem(l, name), 16)

            for l in range(DEPTH):
                T = span(l)
                S = lambda name, l=l: sem(l, name)
                if l > 0:
                    pool.wait_ge(sem("all", "layer_done"), l)
                    pool.sem_inc(sem("all", "passed"), 1)
                HALF = KT * TOK // 2
                pool.wait_ge(S("zr"), first_tile[at["gate", 0]])
                pool.wait_ge(S("spill"), 16)
                load(l, "x_back", xT[:, 0:KT // 2, :], x_spill[:, 0:HALF])
                for t in range(KT):
                    pool.wait_ge(S("m_hi"), t + 1)
                    nc.gpsimd.tensor_tensor(m_lo[:, t, 0:T], merged[:, t, 0:T], m_hi[:, t, 0:T].bitcast(f32), SUB).then_inc(S("m_lo"), 1)
                pool.wait_ge(S("zr"), first_tile[at["out", 0]])
                load(l, "x_back2", xT[:, KT // 2:, :], x_spill[:, HALF:])
                load(l, "x_back2", wr[:, :, :], A["w_router"].rearrange("(k p) n -> p k n", p=P))
                if l == 0:
                    pool.wait_ge(sem("all", "y_zeroed"), (NI - NE) * 16)
                pool.wait_ge(S("rows_ok"), 1)
                for t in range(T // P):
                    for c in range(2):
                        pool.indirect_dma_start(
                            out=yg[:, t, c, :], out_offset=None, in_=y_rows,
                            in_offset=bass.IndirectOffsetOnAxis(ap=rowid[:, 2 * t + c:2 * t + c + 1], axis=0),
                        ).then_inc(S(f"yg{t // 2}"), 16)
                pool.sem_inc(sem("all", "engine_done"), 1)

        @block.scalar
        def _(act):
            a = Program(act, "act_steps")

            def fn(out_, in_, f, **kw):
                return nc.scalar.activation(out_, in_, f, **kw)

            def load(l, name, dst, src):
                act.dma_start(dst, src).then_inc(sem(l, name), 16)

            for l in range(DEPTH):
                T = span(l)
                NS = seqs(l)
                NF = 3 if NS == 2 else 2
                F0 = 0 if l == 0 else 4
                S = lambda name, l=l: sem(l, name)

                def split(n):
                    act.wait_ge(sem("all", f"w{n % RING}"), 16 * (l * len(range(n % RING, NU, RING)) + n // RING + 1))
                    if n >= RING:
                        act.wait_ge(S("zr"), first_tile[n - RING + 1])
                    fn(whi[n % RING][:, :], stage[n % RING][:, :], ACT.Copy).then_inc(S("hi"), 1)

                def tile_ready(m):
                    act.wait_ge(S("zr"), m + 1)

                def z(m):
                    return bank[m % 2]

                if l > 0:
                    act.wait_ge(sem("all", "layer_done"), l)
                    act.sem_inc(sem("all", "passed"), 1)
                if l == 0:
                    load("all", "x_in", xrow[:, 0:2, :], A["x"][0].rearrange("(t p) n -> p t n", p=P))
                    load("all", "x_in", xrow[:, 2:4, :], A["ctx"][0].rearrange("(t p) n -> p t n", p=P))
                if l == 0:
                    small_loads(act, 0)
                if l == 0:
                    act.wait_ge(sem("all", "c_in"), 48)
                    fn(crow_s[:, :], crow[:, :], ACT.Silu).then_inc(sem("all", "c_silu"), 1)
                    act.wait_ge(sem("all", "cT"), 1)
                    act.wait_ge(sem("all", "cst_zero"), 1)
                    fn(cst[:, :, 0:2], bank[1][:, 0:16].rearrange("p (s k) -> p k s", s=2), ACT.Copy).then_inc(sem("all", "c_hi"), 1)
                    for k in range(0, KT, 2):
                        act.wait_ge(sem("all", "xt"), k + 1)
                        fn(xT[:, k, :], bank[k][:, :], ACT.Copy).then_inc(sem("all", "xt_act"), 1)
                def squares(k0, k1):
                    for k in range(k0, k1):
                        mk = first_tile[at["out", 0]] + k
                        act.wait_ge(S(f"zf{mk % 2}"), mk // 2 + 1)
                        if k >= 2:
                            act.wait_ge(S("n2_stat"), k - 1)
                        fn(sq[:, k % 2, 0:T], xT[:, k, 0:T], ACT.Square).then_inc(S("n2_sq"), 1)

                split(0)
                split(1)
                for n, (kind, j) in enumerate(units):
                    m = first_tile[n]
                    if n + 2 < NU:
                        split(n + 2)
                    if kind == "out" and j >= 1:
                        squares(2 * j - 2, 2 * j)
                    if kind == "mod":
                        tile_ready(m)
                        if j >= 2:
                            act.wait_ge(S("modcol"), j - 1)
                        fn(modrow[:, j % 2, :], z(m)[0:4, 0:UW], ACT.Copy).then_inc(S(f"zf{m % 2}"), 1)
                    if n - F0 in (2, 4):
                        i = (n - F0) // 2 - 1
                        act.wait_ge(S("f_arg"), i + 1)
                        fn(fh[:, i, :], fh[:, i, :], ACT.Sin).then_inc(S("f_sin"), 1)
                    if n in (0, 1):
                        for k in range(4 * n, 4 * n + 4):
                            if l == 0:
                                act.wait_ge(sem("all", "xt_dve" if k % 2 else "xt_act"), k // 2 + 1)
                            fn(sq1[:, k, :], xT[:, k, :], ACT.Square).then_inc(S("n1_sq"), 1)
                    if n == F0 + 6:
                        for t in range(2):
                            act.wait_ge(S("f_raw"), t + 1)
                            fn(habs[:, t, :], hfil[:, t, :], ACT.Abs).then_inc(S("f_abs"), 1)
                    if 0 <= n - H_SLOT < KT:
                        k = n - H_SLOT
                        act.wait_ge(S("hn"), k + 1)
                        if k >= 2:
                            act.wait_ge(S("h_lo"), k - 1)
                        for s in range(2):
                            c = slice(s * SEQ, (s + 1) * SEQ)
                            fn(hm[:, k % 2, c], hn[:, k % 2, c], ACT.Identity, scale=amp[:, 0, k, s:s + 1],
                               bias=modT[:, 2 * k + s:2 * k + s + 1]).then_inc(S("hm"), 1)
                        act.wait_ge(S("hm"), 2 * (k + 1))
                        fn(h_hi[:, k, :], hm[:, k % 2, :], ACT.Copy).then_inc(S("h_hi"), 1)
                    if kind == "in" and j < 2:
                        for t in range(2):
                            i = 2 * j + t
                            tile_ready(m + t)
                            fn(zraw[:, i, 0:T], z(m + t)[:, 0:T], ACT.Copy).then_inc(S(f"zf{(m + t) % 2}"), 1)
                            act.wait_ge(S(f"zf{(m + t) % 2}"), (m + t) // 2 + 1)
                            fn(zsq[:, i, 0:T], zraw[:, i, 0:T], ACT.Square).then_inc(S("q_sq"), 1)
                    if n == 4:
                        act.wait_ge(S("mean_sq"), 1)
                        fn(rs[:, :], rs[:, :], ACT.Sqrt).then_inc(S("root"), 1)
                    if kind == "in" and j == 2:
                        tile_ready(m)
                        fn(kraw[:, :], z(m)[:, :], ACT.Copy).then_inc(S(f"zf{m % 2}"), 1)
                        act.wait_ge(S(f"zf{m % 2}"), m // 2 + 1)
                        fn(ksq[:, :], kraw[:, :], ACT.Square).then_inc(S("k_sq"), 1)
                        tile_ready(m + 1)
                        fn(vT[:, :], z(m + 1)[:, :], ACT.Copy).then_inc(S(f"zf{(m + 1) % 2}"), 1)
                    if n == Q_SLOT + 1:
                        act.wait_ge(S("mean_sq"), 2)
                        NQ = (T // P) * NH
                        fl = rsq[:, :, :].rearrange("p t h -> p (t h)")
                        fn(fl[:, 0:NQ], fl[:, 0:NQ], ACT.Sqrt).then_inc(S("root"), 1)
                    if n == K_SLOT:
                        act.wait_ge(S("vrows"), 1)
                        fn(vr[:, :, :].rearrange("p t n -> p (t n)"), bank[5][:, :], ACT.Copy).then_inc(S("v_ok"), 1)
                    if kind == "in" and 3 <= j < 6:
                        for t in range(2):
                            i = 2 * (j - 3) + t
                            tile_ready(m + t)
                            if i >= 4:
                                act.wait_ge(S("short"), i - 3)
                            if i < 4:
                                act.wait_ge(S("q_ok"), 4)
                            fn(zraw[:, i % 4, 0:T], z(m + t)[:, 0:T], ACT.Copy).then_inc(S(f"zf{(m + t) % 2}"), 1)
                    if n == K_SLOT + 1:
                        act.wait_ge(S("mean_sq"), 3)
                        fn(krs[:, :], krs[:, :], ACT.Sqrt).then_inc(S("root"), 1)
                    if n == U_SLOT:
                        act.wait_ge(S("uT"), 1)
                        fn(urow[:, 0, 0:T], bank[5][:, 0:T], ACT.Copy).then_inc(S("u_act"), 1)
                    if kind == "in" and j >= 6:
                        for t in range(2):
                            tile_ready(m + t)
                            src = z(m + t)[:, 0:T].rearrange("p (s n) -> p s n", s=NS)
                            if j == 6:
                                act.wait_ge(S("glu_free"), 1)
                                fn(glu[:, t, 0:NS, 15:15 + SEQ], src, ACT.Copy).then_inc(S(f"zf{(m + t) % 2}"), 1)
                            else:
                                fn(gsig[:, t, 0:T], z(m + t)[:, 0:T], ACT.Sigmoid).then_inc(S(f"zf{(m + t) % 2}"), 1)
                    if n == at["mod", 23]:
                        for t in range(2):
                            act.wait_ge(S("hy_o"), t + 1)
                            fn(oh_hi[:, t, 0:T], hyo[:, t, 0:T], ACT.Copy).then_inc(S("oh_hi"), 1)

                    i = n - HEAD0
                    if 1 <= i <= NH:
                        act.wait_ge(S("pT"), NF * (i - 1) + 1)
                        if i >= 2:
                            act.wait_ge(S("pv"), i - 1)
                        fn(pT[:, 0, :], bank[5][:, :], ACT.Copy).then_inc(S("pT_act"), 1)
                    if kind == "gate":
                        for t in range(2):
                            tile_ready(m + t)
                            g = 2 * (j % 4) + t
                            if n < at["gate", 0] and j == 4 and t == 0:
                                act.wait_ge(S("glu_ok"), 2)
                                act.wait_ge(S("oh_lo"), 2)
                            if 0 <= j < 4:
                                act.wait_ge(S("mg_h"), g + 1)
                            if j >= 8:
                                act.wait_ge(S("mg_a"), g + 1)
                            fn(gates[:, g, 0:T], z(m + t)[:, 0:T], ACT.Sigmoid).then_inc(S(f"zf{(m + t) % 2}"), 1)
                    if 1 <= i <= NH and NS == 2:
                        act.wait_ge(S("pT"), NF * i)
                        fn(pT[:, 2, :], bank[5][:, :], ACT.Copy).then_inc(S("pT_act"), 1)
                    if 0 <= i < NH:
                        act.wait_ge(S("nmax"), i + 1)
                        if i >= 1:
                            act.wait_ge(S("pT"), NF * i)
                        for c in range(T // P):
                            src = bank[2 + c][:, :] if c < 2 else bank[4][:, (c - 2) * 256:(c - 1) * 256]
                            dst = probs[:, c, :] if c < 2 else probs[:, 2, (c - 2) * 256:(c - 1) * 256]
                            ins = fn(dst, src, ACT.Exp, bias=small[:, 4 + c:5 + c], scale=rsq[:, c, i:i + 1],
                                     accum_out=small[:, 8 + c:9 + c])
                            ins.then_inc(S("exp"), 1)
                    if 1 <= i <= NH:
                        if i % 2 == 0:
                            act.wait_ge(S("pv"), i)
                            fn(oa_hi[:, i // 2 - 1, 0:T], bank[7][:, 0:T], ACT.Copy).then_inc(S("oa_hi"), 1)
                    if n == at["gate", 8]:
                        for t in range(2):
                            act.wait_ge(S("cf_xc"), t + 1)
                            fn(csq[:, t, 0:T], conv[:, t, 0:T], ACT.Square).then_inc(S("cf_sq"), 1)
                    if n == at["gate", 9]:
                        act.wait_ge(S("mean_sq"), 4)
                        fn(crs[:, 0:T], crs[:, 0:T], ACT.Sqrt).then_inc(S("root"), 1)
                    if n == at["gate", 10]:
                        for t in range(2):
                            act.wait_ge(S("cf_n"), t + 1)
                            fn(co[:, t, 0:T], conv[:, t, 0:T], ACT.Silu, scale=vec[:, 90 + t:91 + t],
                               bias=vec[:, 92 + t:93 + t]).then_inc(S("cf_o"), 1)
                            act.wait_ge(S("cf_o"), t + 1)
                            fn(oc_hi[:, t, 0:T], co[:, t, 0:T], ACT.Copy).then_inc(S("oc_hi"), 1)
                    if kind == "proj_c":
                        for t in range(KT):
                            act.wait_ge(S("mg_c"), t + 1)
                            fn(m_hi[:, t, 0:T], merged[:, t, 0:T], ACT.Copy).then_inc(S("m_hi"), 1)

                squares(KT - 2, KT)
                act.wait_ge(S("mean_sq"), 5)
                fn(rs[:, 0:T], rs[:, 0:T], ACT.Sqrt).then_inc(S("root"), 1)
                act.wait_ge(S("zr"), total)
                act.sem_inc(S("e_hi"), EW)
                act.sem_inc(S("y_out"), 16)
                NT = T // P

                def rows_high(b):
                    t, c = b % NT, b // NT
                    act.wait_ge(S("rows"), b + 1)
                    fn(t_hi[:, t, c * 512:(c + 1) * 512], row_bank(b)[:, :], ACT.Copy).then_inc(S("row_hi"), 1)

                for k in range(KT):
                    act.wait_ge(S("hn"), KT + k + 1)
                    for s in range(NS):
                        c = slice(s * SEQ, (s + 1) * SEQ)
                        fn(h2T[:, k, c], hn[:, k % 2, c], ACT.Identity, scale=amp[:, 1, k, s:s + 1],
                           bias=modT[:, 48 + 2 * k + s:49 + 2 * k + s]).then_inc(S("h2"), 1)
                    if 4 <= k < 4 + NT:
                        rows_high(k - 4)
                act.wait_ge(S("lg"), 1)
                fn(lgT[:, 0:T], bank[7][0:NE, 0:T], ACT.Copy).then_inc(S("lgT"), 1)
                rows_high(NT)
                act.wait_ge(S("logits"), 1)
                fn(rt[:, 0, 0:NT * NE], bank[7][:, 0:NT * NE], ACT.Sigmoid).then_inc(S("affin"), 1)
                for b in range(NT + 1, 2 * NT):
                    rows_high(b)

                def esplit(i, j):
                    act.wait_ge(S(f"ew{j}"), (i + 1) * 16)
                    act.wait_ge(S("e_used"), i * EW + j + 1)
                    fn(half_unit(whi, j % EP), estage(j), ACT.Copy).then_inc(S("e_hi"), 1)

                def gathered(i):
                    act.wait_ge(S("e_used"), i * EW - 4 + EP)
                    for c in range(2):
                        act.wait_ge(S("g_cols"), i * 2 + c + 1)
                        fn(xg_hi[:, 4 * c:4 * c + 4, :].rearrange("p k n -> p (k n)"), bank[4 + c][:, :], ACT.Copy).then_inc(S("xg_hi"), 1)

                def picked(i):
                    act.wait_ge(S("g_rows"), i * 2 + 3)
                    fn(xpick[:, 0:512], bank[2][:, :], ACT.Copy).then_inc(S("xr_a"), 1)

                def y_evac(i):
                    act.wait_ge(S("y_out"), i * 16 + 16)
                    act.wait_ge(S("e_used"), i * EW + EP)
                    for c in range(2):
                        ins = fn(yrow[:, c * 512:(c + 1) * 512], bank[6 + c][:, :], ACT.Copy)
                    ins.then_inc(S("e_yev"), 1)

                def item(i, more):
                    y_evac(i)
                    for j in range(6, 10):
                        esplit(i, j)
                    act.wait_ge(S("e_used"), i * EW + 4 + EP)
                    fn(act_s[:, :], bank[0][:, :], ACT.Silu).then_inc(S("silu"), 1)
                    esplit(i, 10)
                    esplit(i, 11)
                    if more:
                        esplit(i + 1, 0)
                        gathered(i + 1)
                    act.wait_ge(S("aT"), i + 1)
                    fn(a_hi[:, :, :].rearrange("p k n -> p (k n)"), bank[0][:, :], ACT.Copy).then_inc(S("a_hi"), 1)
                    if more:
                        picked(i + 2)
                        for j in range(1, 6):
                            esplit(i + 1, j)

                for j in range(6):
                    esplit(0, j)
                act.wait_ge(S("items_ok"), 1)
                last = act.value_load(items_i[0:1, NI:NI + 1], min_val=NE - 1, max_val=NI - 1)
                picked(0)
                gathered(0)
                picked(1)
                with act.Fori(0, last) as i:
                    item(i, True)
                item(last, False)
                y_evac(last + 1)
                act.sem_inc(sem("all", "engine_done"), 1)
                if l == DEPTH - 1:
                    for t in range(2):
                        act.wait_ge(sem("all", "orow_ok"), 2 * (t + 1))
                        act.dma_start(out[0, t * P:(t + 1) * P, :], orow[:, t, :]).then_inc(sem("all", "rows_out"), 16)
                    act.wait_ge(sem("all", "rows_out"), 32)

        @block.vector
        def _(dve):
            v = Program(dve, "dve_steps")
            V = nc.vector

            def tt(o, x, y, op):
                return V.tensor_tensor(o, x, y, op)

            def ts(o, x, s1, s2, op0, op1=None):
                return V.tensor_scalar(o, x, s1, s2, op0, op1) if op1 is not None else V.tensor_scalar(o, x, s1, None, op0)

            def stt(o, x, s, y, op0, op1):
                return V.scalar_tensor_tensor(out=o, in0=x, scalar=s, in1=y, op0=op0, op1=op1)

            V.memset(cst[:, :, :].bitcast(f32), 0.0).then_inc(sem("all", "cst_zero"), 1)
            V.memset(zero_rows[:, :], 0.0).then_inc(sem("all", "zeros"), 1)
            v.then(V.memset(glu[:, :, :, :], 0.0))
            dve.wait_ge(sem("all", "const_in"), 11 * 16)
            for l in range(DEPTH):
                T = span(l)
                NS = seqs(l)
                NF = 3 if NS == 2 else 2
                F0 = 0 if l == 0 else 4
                NT = T // P
                S = lambda name, l=l: sem(l, name)

                def split(n):
                    dve.wait_ge(S("hi"), n + 1)
                    if n >= RING:
                        dve.wait_ge(S("zr"), first_tile[n - RING + 1])
                    tt(wlo[n % RING][:, :], stage[n % RING][:, :], whi[n % RING][:, :].bitcast(f32), SUB).then_inc(S("lo"), 1)

                def tile_ready(m):
                    dve.wait_ge(S("zr"), m + 1)

                def z(m):
                    return bank[m % 2]

                def vcol(c):
                    return vec[:, c:c + 1]

                def modulation(half):
                    lo_, hi_ = (0, 32) if half == 0 else (32, 96)
                    dve.wait_ge(S("modcol"), 8 if half == 0 else 24)
                    b = vec[:, lo_ // 2:hi_ // 2].unsqueeze(2).to_broadcast([P, (hi_ - lo_) // 2, 2])
                    v.then(tt(modT[:, lo_:hi_].rearrange("p (c s) -> p c s", s=2), bank[7][:, lo_:hi_].rearrange("p (c s) -> p c s", s=2), b, ADD))
                    sc = (16, 64)[half]
                    g = vec[:, 48 + 8 * half:56 + 8 * half].unsqueeze(2).to_broadcast([P, KT, 2])
                    src = modT[:, sc:sc + 16].rearrange("p (k s) -> p k s", s=2)
                    v.then(ts(amp[:, half, :, :], src, 1.0, None, ADD))
                    v.then(tt(amp[:, half, :, :], amp[:, half, :, :], g, MUL))

                def shift(chunk, k, s):
                    c = chunk * 16 + 2 * k + s
                    return modT[:, c:c + 1]

                def inverse_rms(name, T_, bnk):
                    dve.wait_ge(S(f"{name}_stat"), KT)
                    ts(rs[:, 0:T_], bnk[:, 0:T_], 1.0 / D, EPS, MUL, ADD).then_inc(S("mean_sq"), 1)
                    dve.wait_ge(S("root"), 1 if name == "n1" else 5)
                    v.then(V.reciprocal(rs[:, 0:T_], rs[:, 0:T_]))

                if l > 0:
                    dve.wait_ge(sem("all", "layer_done"), l)
                    dve.sem_inc(sem("all", "passed"), 1)
                dve.sem_inc(S("glu_free"), 1)
                v.then(V.memset(vrow1[:, :], 0.0))
                V.memset(vrow2[:, :], 0.0).then_inc(S("vec_zero"), 1)

                def vectors():
                    dve.wait_ge(S("vecT"), 1)
                    V.tensor_copy(vec[:, :], bank[6][:, 0:NVEC1 + NVEC2]).then_inc(S("vec_ok"), 1)

                if l == 0:
                    vectors()
                if l == 0:
                    dve.wait_ge(sem("all", "c_hi"), 1)
                    tt(cst[:, :, 2:4], bank[1][:, 0:16].rearrange("p (s k) -> p k s", s=2), cst[:, :, 0:2].bitcast(f32), SUB).then_inc(sem("all", "c_lo"), 1)
                    for k in range(1, KT, 2):
                        dve.wait_ge(sem("all", "xt"), k + 1)
                        V.tensor_copy(xT[:, k, :], bank[k][:, :]).then_inc(sem("all", "xt_dve"), 1)

                def sine_argument(i):
                    dve.wait_ge(S("f_mm"), i + 1)
                    dve.wait_ge(S("vec_ok"), 1)
                    f, n_ = fh[:, i, :], habs[0:64, 0, 0:SEQ]
                    v.then(ts(f, bank[3][0:64, 0:SEQ], vec[0:64, 96 + i:97 + i], vec[0:64, 98:99], ADD, MUL))
                    v.then(ts(n_, f, 1.0 / (2 * math.pi), ROUND, MUL, ADD))
                    v.then(ts(n_, n_, ROUND, None, SUB))
                    v.then(stt(f, n_, -TWO_PI_HI, f, MUL, ADD))
                    v.then(stt(f, n_, -TWO_PI_LO, f, MUL, ADD))
                    ts(f, f, PI, -PI, ALU.min, ALU.max).then_inc(S("f_arg"), 1)

                def taps(k0, k1):
                    for k in range(k0, min(k1, 31)):
                        for t in range(2):
                            src = glu[:, t, 0:NS, k:k + SEQ]
                            dst = conv[:, t, 0:T].rearrange("p (s n) -> p s n", s=NS)
                            w = vcol(NVEC1 + 2 * k + t)
                            if k == 0:
                                v.step(ts(dst, src, w, vcol(88 + t), MUL, ADD))
                            else:
                                dve.wait_ge(v.steps, v.count - 1)
                                v.step(stt(dst, src, w, dst, MUL, ADD))
                    v.sync()

                split(0)
                split(1)
                taps_done = 0
                for n, (kind, j) in enumerate(units):
                    m = first_tile[n]
                    if n == H_SLOT:
                        modulation(0)
                        dve.sem_inc(S("mod_done"), 1)
                    if 0 <= n - H_SLOT < KT:
                        k = n - H_SLOT
                        if k >= 2:
                            dve.wait_ge(S("hm"), 2 * (k - 1))
                        tt(hn[:, k % 2, :], xT[:, k, :], rs[:, :], MUL).then_inc(S("hn"), 1)
                    if n + 2 < NU and kind not in ("proj_h", "proj_a", "proj_c"):
                        split(n + 2)
                    if n == F0 and l > 0:
                        vectors()
                    if n - F0 in (1, 3):
                        sine_argument((n - F0) // 2)
                    if n == F0 + 5:
                        dve.wait_ge(S("fil2_in"), 32)
                        for t in range(2):
                            dve.wait_ge(S("f_mm"), 3 + t)
                            tt(hfil[:, t, :], bank[4 + t][:, :], decay[:, t, :], MUL).then_inc(S("f_raw"), 1)
                    if n == at["mod", 16]:
                        dve.wait_ge(S("f_mm"), 5)
                        v.then(V.reciprocal(hinv[:, :], bank[6][:, :]))
                        for t in range(2):
                            v.then(tt(hfil[:, t, :], hfil[:, t, :], hinv[:, :], MUL))
                        v.then(V.memset(hfil[0:1, 0, SEQ:2 * SEQ], 0.0))
                        v.step(tt(hs[:, :, :], hfil[:, :, 0:SEQ], hfil[:, :, SEQ:2 * SEQ], ADD))
                        tt(hd[:, :, :], hfil[:, :, 0:SEQ], hfil[:, :, SEQ:2 * SEQ], SUB).then_inc(S("f_sd"), 1)
                    if n == 4:
                        inverse_rms("n1", TOK, bank[2])
                    if n == at["mod", 19]:
                        dve.wait_ge(S("f_mm"), 6)
                        v.step(V.tensor_copy(H[:, 0, :, :].rearrange("p f n -> p (f n)"), bank[3][:, :]))
                        V.tensor_copy(H[:, 1, :, :].rearrange("p f n -> p (f n)"), bank[4][:, :]).then_inc(S("H_ok"), 1)
                    if 1 <= n - H_SLOT <= KT:
                        k = n - H_SLOT
                        dve.wait_ge(S("h_hi"), k)
                        tt(h_lo[:, k - 1, :], hm[:, (k - 1) % 2, :], h_hi[:, k - 1, :].bitcast(f32), SUB).then_inc(S("h_lo"), 1)
                    if kind == "in" and j < 2:
                        for t in range(2):
                            i = 2 * j + t
                            dve.wait_ge(S(f"zf{(m + t) % 2}"), (m + t) // 2 + 1)
                            if i == 0:
                                dve.wait_ge(S("h_lo"), KT)
                            ts(q[:, i, 0:T], zraw[:, i, 0:T], vcol(94), None, MUL).then_inc(S("q_g"), 1)
                    if n == Q_SLOT:
                        dve.wait_ge(S("q_stat"), 1)
                        NQ = NT * NH
                        fl = rsq[:, :, :].rearrange("p t h -> p (t h)")
                        ts(fl[:, 0:NQ], bank[5][:, 0:NQ], 1.0, 64.0 * EPS, MUL, ADD).then_inc(S("mean_sq"), 1)
                    if n == Q_SLOT + 1:
                        dve.wait_ge(S("root"), 2)
                        v.then(V.reciprocal(fl[:, 0:NQ], fl[:, 0:NQ]))
                        for i in range(4):
                            dve.wait_ge(S("q_rot"), 4)
                            dve.wait_ge(S("q_g"), i + 1)
                            v.then(tt(ropet[:, i % 2, :], bank[2 + i // 2][:, (i % 2) * SEQ:(i % 2 + 1) * SEQ], sinT[:, :], MUL))
                            v.then(tt(q[:, i, 0:SEQ], q[:, i, 0:SEQ], cosT[:, :], MUL))
                            tt(q[:, i, 0:SEQ], q[:, i, 0:SEQ], ropet[:, i % 2, :], ADD).then_inc(S("q_ok"), 1)
                    if n == K_SLOT:
                        dve.wait_ge(S("k_stat"), 1)
                        ts(krs[:, :], bank[4][:, :], EPS, None, ADD).then_inc(S("mean_sq"), 1)
                    if n == K_SLOT + 1:
                        dve.wait_ge(S("root"), 3)
                        v.then(V.reciprocal(krs[:, :], krs[:, :]))
                        v.then(tt(kraw[:, :], kraw[:, :], krs[:, :], MUL))
                        ts(kraw[:, :], kraw[:, :], vcol(95), None, MUL).then_inc(S("k_g"), 1)
                    if n == KROT_SLOT + 1:
                        dve.wait_ge(S("k_rot"), 1)
                        v.then(tt(ropet[:, 0, :], bank[4][:, 0:SEQ], sinT[:, :], MUL))
                        v.then(tt(kraw[:, 0:SEQ], kraw[:, 0:SEQ], cosT[:, :], MUL))
                        v.then(tt(kraw[:, 0:SEQ], kraw[:, 0:SEQ], ropet[:, 0, :], ADD))
                        if l == 0:
                            dve.wait_ge(sem("all", "y_zeroed"), (NI - NE) * 16)
                        for g in range(2):
                            for h in range(2):
                                ins = V.tensor_copy(kd[64 * h:64 * h + 64, g, :], kraw[64 * g:64 * g + 64, :])
                                if (g, h) != (1, 1):
                                    v.step(ins)
                        ins.then_inc(S("k_ok"), 1)
                    if kind == "in" and 3 <= j < 6:
                        for t in range(2):
                            i = 2 * (j - 3) + t
                            dve.wait_ge(S(f"zf{(m + t) % 2}"), (m + t) // 2 + 1)
                            src = zraw[:, i % 4, 0:T].rearrange("p (s n) -> p s n", s=NS)
                            dst = zhy[:, i, 0:T].rearrange("p (s n) -> p s n", s=NS)
                            v.then(ts(dst, src, vcol(64 + 6 + i), vcol(82 + i), MUL, ADD))
                            v.then(stt(dst[:, :, 1:SEQ], src[:, :, 0:SEQ - 1], vcol(64 + i), dst[:, :, 1:SEQ], MUL, ADD))
                            stt(dst[:, :, 0:SEQ - 1], src[:, :, 1:SEQ], vcol(64 + 12 + i), dst[:, :, 0:SEQ - 1], MUL, ADD).then_inc(S("short"), 1)
                        if j == 5:
                            for t in range(2):
                                dve.wait_ge(S("short"), 5 + t)
                                tt(zhy[:, 2 + t, 0:T], zhy[:, 4 + t, 0:T], zhy[:, 2 + t, 0:T], MUL).then_inc(S("u"), 1)
                    if n == U_SLOT:
                        dve.wait_ge(S("uT"), 2)
                        V.tensor_copy(urow[:, 1, 0:T], bank[6][:, 0:T]).then_inc(S("u_dve"), 1)
                    if n == at["in", 6]:
                        for f in range(2):
                            dve.wait_ge(S("U"), 2 * (f + 1))
                            ur, ui = bank[2 + 2 * f], bank[3 + 2 * f]
                            for s in range(NS):
                                c = slice(s * SEQ, (s + 1) * SEQ)
                                v.step(tt(ytmp[:, 0, c], ur[:, c], H[:, 0, f, :], MUL))
                                v.then(tt(ytmp[:, 1, c], ui[:, c], H[:, 1, f, :], MUL))
                                v.then(tt(Y[:, 0, f, c], ytmp[:, 0, c], ytmp[:, 1, c], SUB))
                                v.step(tt(ytmp[:, 0, c], ur[:, c], H[:, 1, f, :], MUL))
                                v.then(tt(ytmp[:, 1, c], ui[:, c], H[:, 0, f, :], MUL))
                                tt(Y[:, 1, f, c], ytmp[:, 0, c], ytmp[:, 1, c], ADD).then_inc(S("Y"), 1)
                                dve.wait_ge(S("Y"), f * NS + s + 1)
                    if n == at["in", 7]:
                        for t in range(2):
                            dve.wait_ge(S(f"zf{(m + t) % 2}"), (m + t) // 2 + 1)
                            g = glu[:, t, 0:NS, 15:15 + SEQ]
                            tt(g, g, gsig[:, t, 0:T].rearrange("p (s n) -> p s n", s=NS), MUL).then_inc(S("glu_ok"), 1)
                        dve.wait_ge(S("glu_ok"), 2)
                    if n == at["mod", 23]:
                        for t in range(2):
                            dve.wait_ge(S("y_hy"), t + 1)
                            tt(hyo[:, t, 0:T], bank[5 + t][:, 0:T], zhy[:, t, 0:T], MUL).then_inc(S("hy_o"), 1)
                            dve.wait_ge(S("oh_hi"), t + 1)
                            tt(oh_lo[:, t, 0:T], hyo[:, t, 0:T], oh_hi[:, t, 0:T].bitcast(f32), SUB).then_inc(S("oh_lo"), 1)
                        modulation(1)
                        dve.sem_inc(S("mod_done"), 1)

                    if kind in ("proj_h", "proj_a", "proj_c"):
                        mg = first_tile[at["gate", {"proj_h": 7, "proj_a": 3, "proj_c": 11}[kind]]]
                        for t in range(2):
                            dve.wait_ge(S(f"zf{(mg + t) % 2}"), (mg + t) // 2 + 1)
                        for t in range(n_tiles[kind]):
                            g = 4 * j + t
                            tile_ready(m + t)
                            zt = z(m + t)[:, 0:T]
                            free = S(f"zf{(m + t) % 2}")
                            if kind == "proj_h":
                                tt(merged[:, g, 0:T], gates[:, g, 0:T], zt, MUL).then_inc(free, 1)
                                dve.wait_ge(free, (m + t) // 2 + 1)
                                dve.sem_inc(S("mg_h"), 1)
                            else:
                                tt(gates[:, g, 0:T], gates[:, g, 0:T], zt, MUL).then_inc(free, 1)
                                dve.wait_ge(free, (m + t) // 2 + 1)
                                tt(merged[:, g, 0:T], merged[:, g, 0:T], gates[:, g, 0:T], ADD).then_inc(S("mg_a" if kind == "proj_a" else "mg_c"), 1)
                    if kind in ("proj_h", "proj_a", "proj_c"):
                        split(n + 2)

                    i = n - HEAD0
                    if 1 <= i <= NH:
                        dve.wait_ge(S("pT"), NF * (i - 1) + 2)
                        if i >= 2:
                            dve.wait_ge(S("pv"), i - 1)
                        V.tensor_copy(pT[:, 1, :], bank[6][:, :]).then_inc(S("pT_dve"), 1)
                    if 0 <= i < NH:
                        dve.wait_ge(S("score"), i + 1)
                        v.step(V.reduce_max(small[:, 0:1], bank[2][:, :], AX.X))
                        v.step(V.reduce_max(small[:, 1:2], bank[3][:, :], AX.X))
                        if NS == 2:
                            v.step(V.reduce_max(small[:, 2:4], bank[4][:, :].rearrange("p (c n) -> p c n", c=2), AX.X))
                        v.sync()
                        stt(small[:, 4:4 + NT], small[:, 0:NT], -1.0, rsq[:, 0:NT, i], MUL, MUL).then_inc(S("nmax"), 1)
                        dve.wait_ge(S("exp"), NT * (i + 1))
                        v.then(V.reciprocal(small[:, 12:12 + NT], small[:, 8:8 + NT]))
                        for c in range(NT):
                            p_ = probs[:, c, :] if c < 2 else probs[:, 2, (c - 2) * 256:(c - 1) * 256]
                            ts(p_, p_, small[:, 12 + c:13 + c], None, MUL).then_inc(S("probs"), 1)
                    if 1 <= i <= NH and i % 2 == 0:
                        dve.wait_ge(S("oa_hi"), i // 2)
                        tt(oa_lo[:, i // 2 - 1, 0:T], bank[7][:, 0:T], oa_hi[:, i // 2 - 1, 0:T].bitcast(f32), SUB).then_inc(S("oa_lo"), 1)
                    if at["in", 7] <= n < at["gate", 8] and n + 1 != at["proj_h", 0] and taps_done < 31:
                        more = 2 if n < FIRST_GATE else 4
                        taps(taps_done, taps_done + more)
                        taps_done = min(31, taps_done + more)
                        if taps_done == 31:
                            dve.sem_inc(S("conv_ok"), 1)
                    if n == at["gate", 8]:
                        dve.wait_ge(S("cf_mean"), 1)
                        for t in range(2):
                            stt(conv[:, t, 0:T], bank[5][:, 0:T], -1.0 / 256, conv[:, t, 0:T], MUL, ADD).then_inc(S("cf_xc"), 1)
                    if n == at["gate", 9]:
                        dve.wait_ge(S("cf_var"), 1)
                        ts(crs[:, 0:T], bank[6][:, 0:T], 1.0 / 256, EPS, MUL, ADD).then_inc(S("mean_sq"), 1)
                        dve.wait_ge(S("root"), 4)
                        v.then(V.reciprocal(crs[:, 0:T], crs[:, 0:T]))
                        for t in range(2):
                            tt(conv[:, t, 0:T], conv[:, t, 0:T], crs[:, 0:T], MUL).then_inc(S("cf_n"), 1)
                    if n == at["gate", 10]:
                        for t in range(2):
                            dve.wait_ge(S("oc_hi"), t + 1)
                            tt(oc_lo[:, t, 0:T], co[:, t, 0:T], oc_hi[:, t, 0:T].bitcast(f32), SUB).then_inc(S("oc_lo"), 1)
                    if kind == "out":
                        dve.wait_ge(S("x_back" if j < 2 else "x_back2"), 16 if j < 2 else 32)
                        for t in range(2):
                            k = 2 * j + t
                            tile_ready(m + t)
                            for s in range(NS):
                                c = slice(s * SEQ, (s + 1) * SEQ)
                                ins = stt(xT[:, k, c], z(m + t)[:, c], shift(2, k, s), xT[:, k, c], MUL, ADD)
                                if s < NS - 1:
                                    v.step(ins)
                            ins.then_inc(S(f"zf{(m + t) % 2}"), 1)

                dve.wait_ge(S("zr"), total)
                dve.sem_inc(S("e_lo"), EW)

                def esplit(i, j):
                    dve.wait_ge(S("e_hi"), i * EW + j + 1 + EW)
                    dve.wait_ge(S("e_used"), i * EW + j + 1)
                    tt(half_unit(wlo, j % EP), estage(j), half_unit(whi, j % EP).bitcast(f32), SUB).then_inc(S("e_lo"), 1)

                def rows_low(b):
                    t, c = b % NT, b // NT
                    dve.wait_ge(S("row_hi"), b + 1)
                    tt(t_lo[:, t, c * 512:(c + 1) * 512], row_bank(b)[:, :], t_hi[:, t, c * 512:(c + 1) * 512].bitcast(f32), SUB).then_inc(S("row_lo"), 1)

                inverse_rms("n2", T, bank[2])
                for k in range(KT):
                    if k >= 2:
                        dve.wait_ge(S("h2"), NS * (k - 1))
                    tt(hn[:, k % 2, 0:T], xT[:, k, 0:T], rs[:, 0:T], MUL).then_inc(S("hn"), 1)
                for b in range(NT):
                    rows_low(b)

                W = NT * NE
                dve.wait_ge(sem("all", "c_in"), 48)
                dve.wait_ge(S("affin"), 1)
                aff = rt[:, 0, 0:W]
                e3 = lambda x: x.rearrange("p (t e) -> p t e", e=NE)
                row = lambda i: rt[:, i, 0:W]
                gr = lambda i: grp[:, i, 0:NT * 4]
                sel = row(1)
                v.then(tt(e3(sel), e3(aff), router_b[:, :].unsqueeze(1).to_broadcast([P, NT, NE]), ADD))
                s4 = sel.rearrange("p (g e) -> p g e", e=4)
                a0, a1, a2, a3 = (s4[:, :, c] for c in range(4))
                v.step(tt(gr(0), a0, a1, ALU.max))
                v.step(tt(gr(1), a0, a1, ALU.min))
                v.step(tt(gr(2), a2, a3, ALU.max))
                v.then(tt(gr(3), a2, a3, ALU.min))
                v.step(tt(gr(4), gr(0), gr(2), ALU.max))
                v.step(tt(gr(5), gr(0), gr(2), ALU.min))
                v.then(tt(gr(6), gr(1), gr(3), ALU.max))
                v.then(tt(gr(5), gr(5), gr(6), ALU.max))
                v.then(tt(gr(4), gr(4), gr(5), ADD))
                g3 = lambda x: x.rearrange("p (t g) -> p t g", g=4)

                def pick_first(values, width, order, key, best, view):
                    v.then(V.reduce_max(best, view(values), AX.X))
                    bb = best.unsqueeze(2).to_broadcast([P, NT, width])
                    v.then(tt(view(key), view(values), bb, ALU.is_equal))
                    oo = order.unsqueeze(1).to_broadcast([P, NT, width])
                    v.then(tt(view(key), view(key), oo, MUL))
                    v.then(V.reduce_max(best, view(key), AX.X))
                    v.then(tt(view(key), view(key), bb, ALU.is_equal))

                pick_first(gr(4), 4, first[:, 16:20], gr(6), tokv[:, 0, 0:NT], g3)
                v.then(ts(gr(7), gr(6), 1.0, BIG, SUB, MUL))
                inside = gr(6).unsqueeze(2).to_broadcast([P, NT * 4, 4])
                outside = gr(7).unsqueeze(2).to_broadcast([P, NT * 4, 4])
                m4 = row(2).rearrange("p (g e) -> p g e", e=4)
                v.then(tt(m4, s4, inside, MUL))
                v.then(tt(m4, m4, outside, ADD))
                pick_first(row(2), NE, first[:, 0:16], row(3), tokv[:, 0, 0:NT], e3)
                v.then(stt(row(2), row(3), -BIG, row(2), MUL, ADD))
                pick_first(row(2), NE, first[:, 0:16], row(4), tokv[:, 0, 0:NT], e3)
                v.then(tt(row(5), row(3), row(4), ADD))
                v.then(V.memset(mask_sums[:, 0:NE], 0.0))
                for t in range(NT):
                    ins = tt(mask_sums[:, (t + 1) * NE:(t + 2) * NE], mask_sums[:, t * NE:(t + 1) * NE], rt[:, 5, t * NE:(t + 1) * NE], ADD)
                    if t < NT - 1:
                        v.then(ins)
                ins.then_inc(S("routed"), 1)
                for c in range(2):
                    v.then(tt(row(6), aff, row(3 + c), MUL))
                    v.then(V.reduce_sum(tokv[:, 1 + c, 0:NT], e3(row(6)), AX.X))
                v.then(tt(tokv[:, 3, 0:NT], tokv[:, 1, 0:NT], tokv[:, 2, 0:NT], ADD))
                v.then(V.reciprocal(tokv[:, 3, 0:NT], tokv[:, 3, 0:NT]))
                for c in range(2):
                    v.then(tt(tokv[:, 1 + c, 0:NT], tokv[:, 1 + c, 0:NT], tokv[:, 3, 0:NT], MUL))
                for b in range(NT, 2 * NT):
                    rows_low(b)
                dve.wait_ge(S("places"), 1)
                counts = bank[7][:, 64:64 + NE]
                v.then(ts(chunks[:, :], counts, float(P), 1.0, ALU.is_gt, ADD))
                for c in range(2, TOK // P):
                    v.then(stt(chunks[:, :], counts, float(c * P), chunks[:, :], ALU.is_gt, ADD))
                v.then(V.memset(ends[:, :, :], 0.0))
                v.then(V.tensor_copy(ends[:, 0, 8:], chunks[:, :]))
                for i in range(4):
                    src, dst = ends[:, i % 2, :], ends[:, (i + 1) % 2, :]
                    v.then(tt(dst[:, 8:], src[:, 8:], src[:, 8 - (1 << i):8 - (1 << i) + NE], ADD))
                end = ends[:, 0, 8:]
                v.then(tt(starts[:, :], end, chunks[:, :], SUB))
                it = iota[:, 0:NI].unsqueeze(2).to_broadcast([P, NI, NE])
                v.then(tt(before_end[:, :, :], it, end.unsqueeze(1).to_broadcast([P, NI, NE]), ALU.is_ge))
                v.then(V.reduce_sum(item_f[:, :], before_end[:, :, :], AX.X))
                v.then(V.tensor_copy(items_i[0:1, 0:NI], item_f[0:1, :]))
                ts(items_i[0:1, NI:NI + 1], end[0:1, NE - 1:NE], -1.0, None, ADD).then_inc(S("items_ok"), 1)
                st = starts[:, :].unsqueeze(1).to_broadcast([P, NT, NE])
                v.then(ts(e3(row(6)), st, float(P), None, MUL))
                v.then(tt(row(7), row(6), bank[7][:, 0:W], ADD))
                v.step(V.memset(posm[:, :, :], 0.0))
                v.then(ts(item_base[:, :], iota[:, 0:NI + 1], float(P), -1.0, MUL, ADD))
                ib = item_base[:, :].unsqueeze(1).to_broadcast([P, NT, NI + 1])
                rel = rt[:, 8:10, :].rearrange("p a n -> p (a n)")[:, 0:NT * (NI + 1)].rearrange("p (t i) -> p t i", t=NT)
                for c in range(2):
                    v.then(tt(row(6), row(7), row(3 + c), MUL))
                    v.then(V.reduce_sum(tokv[:, 4 + c, 0:NT], e3(row(6)), AX.X))
                    v.then(tt(rel, tokv[:, 4 + c, 0:NT].unsqueeze(2).to_broadcast([P, NT, NI + 1]), ib, SUB))
                    v.then(stt(rel, rel, float(P), rel, ALU.is_le, MUL))
                    v.then(stt(posm[:, 0:NT, :], rel, 0.0, posm[:, 0:NT, :], ALU.max, ADD))
                    v.then(ts(rowid[:, c:c + 2 * NT - 1:2], tokv[:, 4 + c, 0:NT], float(P), None, ADD))
                v.then(ts(posm[:, :, :], posm[:, :, :], -1.0, None, ADD))

                def picks(i, col):
                    dve.wait_ge(S("g_rows"), i * 2 + 2)
                    for t in range(NT):
                        ins = ts(pick[:, t, :], iota[:, :], posm[:, t, col], None, ALU.is_equal)
                    ins.then_inc(S("pick"), 1)

                def gathered(i, c):
                    dve.wait_ge(S("xg_hi"), i * 2 + c + 1)
                    dst = xg_lo[:, 4 * c:4 * c + 4, :].rearrange("p k n -> p (k n)")
                    hi = xg_hi[:, 4 * c:4 * c + 4, :].rearrange("p k n -> p (k n)").bitcast(f32)
                    tt(dst, bank[4 + c][:, :], hi, SUB).then_inc(S("xg_lo"), 1)

                def picked(i):
                    dve.wait_ge(S("g_rows"), i * 2 + 4)
                    V.tensor_copy(xpick[:, 512:1024], bank[3][:, :]).then_inc(S("xr_d"), 1)

                def item(i, more):
                    esplit(i, 6)
                    if more:
                        picks(i + 2, bass.ds(i + 2, 1))
                    for j in range(7, EW):
                        esplit(i, j)
                    dve.wait_ge(S("silu"), i + 1)
                    dve.wait_ge(S("e_used"), i * EW + 8 + EP)
                    tt(act_a[:, :], act_s[:, :], bank[1][:, :], MUL).then_inc(S("act_a"), 1)
                    if more:
                        esplit(i + 1, 0)
                    dve.wait_ge(S("a_hi"), i + 1)
                    tt(a_lo[:, :, :].rearrange("p k n -> p (k n)"), bank[0][:, :], a_hi[:, :, :].rearrange("p k n -> p (k n)").bitcast(f32), SUB).then_inc(S("a_lo"), 1)
                    if more:
                        gathered(i + 1, 0)
                        gathered(i + 1, 1)
                        esplit(i + 1, 1)
                        picked(i + 2)
                        for j in range(2, 6):
                            esplit(i + 1, j)

                dve.wait_ge(S("items_ok"), 1)
                last = dve.value_load(items_i[0:1, NI:NI + 1], min_val=NE - 1, max_val=NI - 1)
                picks(0, slice(0, 1))
                for j in range(2):
                    esplit(0, j)
                picked(0)
                picks(1, slice(1, 2))
                gathered(0, 0)
                gathered(0, 1)
                picked(1)
                for j in range(2, 6):
                    esplit(0, j)
                with dve.Fori(0, last) as i:
                    item(i, True)
                item(last, False)
                dve.wait_ge(S("y_out"), (last + 3) * 16)
                dve.sem_inc(S("rows_ok"), 1)
                for t in range(NT + 1):
                    if t < NT:
                        dve.wait_ge(S(f"yg{t // 2}"), 4 * 16)
                        if t >= 2:
                            dve.wait_ge(S("combT"), t - 1)
                        v.then(ts(comb[:, t % 2, :], yg[:, t, 0, :], tokv[:, 1, t:t + 1], None, MUL))
                        stt(comb[:, t % 2, :], yg[:, t, 1, :], tokv[:, 2, t:t + 1], comb[:, t % 2, :], MUL, ADD).then_inc(S("combined"), 1)
                    if t >= 1:
                        u = t - 1
                        dve.wait_ge(S("combT"), u + 1)
                        for k in range(KT):
                            b = 2 * (u % 2) + k // 4
                            c_ = slice(u * P, (u + 1) * P)
                            stt(xT[:, k, c_], bank[b][:, (k % 4) * P:(k % 4 + 1) * P], shift(5, k, u // 2), xT[:, k, c_], MUL, ADD).then_inc(S("x_moe"), 1)
                dve.wait_ge(S("x_moe"), NT * KT)
                dve.sem_inc(S("moe_x"), 1)
                if l < DEPTH - 1:
                    dve.wait_ge(sem("all", "engine_done"), 4 * (l + 1))
                    dve.sem_clear(range(numbers[0], numbers[-1] + 1)).then_inc(sem("all", "layer_done"), 1)
                else:
                    for t in range(2):
                        for c in range(2):
                            dve.wait_ge(sem("all", "oT"), 2 * t + c + 1)
                            V.tensor_copy(orow[:, t, c * 512:(c + 1) * 512], bank[2 * t + c][:, :]).then_inc(sem("all", "orow_ok"), 1)
                    dve.sem_inc(sem("all", "layer_done"), 1)

        @block.tensor
        def _(pe):
            MM = nc.tensor.matmul

            def T_(o, i, n=P):
                return nc.tensor.transpose(o, i, ident[0:n, 0:n])

            pe.wait_ge(sem("all", "const_in"), 11 * 16)
            for l in range(DEPTH):
                T = span(l)
                NS = seqs(l)
                NF = 3 if NS == 2 else 2
                F0 = 0 if l == 0 else 4
                NT = T // P
                S = lambda name, l=l: sem(l, name)
                if l > 0:
                    pe.wait_ge(sem("all", "layer_done"), l)
                    pe.sem_inc(sem("all", "passed"), 1)
                def vectors():
                    pe.wait_ge(S("vec_in"), 16 * 16)
                    T_(bank[6][:, 0:NVEC1], vrow1[0:NVEC1, :], NVEC1)
                    T_(bank[6][:, NVEC1:NVEC1 + NVEC2], vrow2[0:NVEC2, :], NVEC2).then_inc(S("vecT"), 1)

                if l == 0:
                    vectors()
                    pe.wait_ge(sem("all", "c_silu"), 1)
                    T_(bank[1][:, 0:16], crow_s[:, :], 16).then_inc(sem("all", "cT"), 1)
                    pe.wait_ge(sem("all", "x_in"), 32)
                    for k in range(KT):
                        if k == 6:
                            pe.wait_ge(S("vec_ok"), 1)
                        if k == 1:
                            pe.wait_ge(sem("all", "c_lo"), 1)
                        for t in range(4):
                            ins = T_(bank[k][:, t * P:(t + 1) * P], xrow[:, t, k * P:(k + 1) * P])
                        ins.then_inc(sem("all", "xt"), 1)
                    pe.wait_ge(sem("all", "xt_act"), 4)
                    pe.wait_ge(sem("all", "xt_dve"), 4)

                def unit_ready(n):
                    pe.wait_ge(S("lo"), n + 1)

                def tile_free(m):
                    if m >= 2:
                        pe.wait_ge(S(f"zf{m % 2}"), m // 2)

                def three(o, w, x_, start, stop):
                    MM(o, w[0], x_[0], start=start, stop=False)
                    MM(o, w[0], x_[1], start=False, stop=False)
                    return MM(o, w[1], x_[0], start=False, stop=stop)

                def mod_columns(jj):
                    mm = first_tile[at["mod", jj]]
                    pe.wait_ge(S(f"zf{mm % 2}"), mm // 2 + 1)
                    if jj == 8:
                        pe.wait_ge(S("mod_done"), 1)
                    for c in range(2):
                        col = (2 * jj + c) * 2
                        ins = MM(bank[7][:, col:col + 2], modrow[:, jj % 2, c * P:(c + 1) * P], fold[:, :], start=True, stop=True)
                    ins.then_inc(S("modcol"), 1)

                def square_sums(k0, k1):
                    for k in range(k0, k1):
                        pe.wait_ge(S("n2_sq"), k + 1)
                        MM(bank[2][:, 0:T], ones[:, :], sq[:, k % 2, 0:T], start=(k == 0), stop=(k == KT - 1)).then_inc(S("n2_stat"), 1)

                mods = 0
                for n, (kind, j) in enumerate(units):
                    m = first_tile[n]
                    unit_ready(n)
                    hi, lo = unit_view(whi[n % RING], n), unit_view(wlo[n % RING], n)
                    if kind == "mod":
                        tile_free(m)
                        if n == 0 and l == 0:
                            pe.wait_ge(sem("all", "c_lo"), 1)
                        for k in range(KT):
                            MM(bank[m % 2][:, 0:UW], cst[:, k, :], hi[:, k, :], start=(k == 0), stop=False)
                            ins = MM(bank[m % 2][:, 0:UW], cst[:, k, :], lo[:, k, :], start=False, stop=(k == KT - 1))
                        ins.then_inc(S("zr"), 1)
                    if kind in ("in", "gate", "out"):
                        if kind == "in" and j == 2:
                            N = TOK
                        else:
                            N = T
                        xh, xl = (m_hi, m_lo) if kind == "out" else (h_hi, h_lo)
                        for t in range(2):
                            tile_free(m + t)
                            for k in range(KT):
                                if n == at["in", 0] and t == 0:
                                    pe.wait_ge(S("h_lo"), k + 1)
                                if n == at["out", 0] and t == 0:
                                    pe.wait_ge(S("m_lo"), k + 1)
                                c = slice(t * P, (t + 1) * P)
                                ins = three(bank[(m + t) % 2][:, 0:N], (hi[:, k, c], lo[:, k, c]), (xh[:, k, 0:N], xl[:, k, 0:N]), k == 0, k == KT - 1)
                            ins.then_inc(S("zr"), 1)
                    if kind in ("proj_h", "proj_a", "proj_c"):
                        xh, xl, nk = {"proj_h": (oh_hi, oh_lo, 2), "proj_a": (oa_hi, oa_lo, 4), "proj_c": (oc_hi, oc_lo, 2)}[kind]
                        name, cnt = {"proj_h": ("oh_lo", 2), "proj_a": ("oa_lo", 4), "proj_c": ("oc_lo", 2)}[kind]
                        pe.wait_ge(S(name), cnt)
                        for t in range(n_tiles[kind]):
                            tile_free(m + t)
                            c = slice(t * P, (t + 1) * P)
                            for k in range(nk):
                                ins = three(bank[(m + t) % 2][:, 0:T], (hi[:, k, c], lo[:, k, c]), (xh[:, k, 0:T], xl[:, k, 0:T]), k == 0, k == nk - 1)
                            ins.then_inc(S("zr"), 1)
                    if n == F0 and l > 0:
                        vectors()
                    if kind == "out" and j >= 1:
                        square_sums(2 * j - 2, 2 * j)
                    upto = sum(1 for u in units[:n + 1] if u[0] == "mod")
                    if not (kind == "mod" and j not in (7, 23)):
                        target = upto
                    else:
                        target = upto - 1
                    while mods < target:
                        mod_columns(mods)
                        mods += 1
                    if n == F0:
                        pe.wait_ge(S("fil_in"), 16 * 5)
                        MM(bank[3][0:64, 0:SEQ], fw1[:, :], feat[:, :], start=True, stop=True).then_inc(S("f_mm"), 1)
                    if n in (1, 2):
                        for k in range(4 * n - 4, 4 * n):
                            pe.wait_ge(S("n1_sq"), k + 1)
                            MM(bank[2][:, :], ones[:, :], sq1[:, k, :], start=(k == 0), stop=(k == KT - 1)).then_inc(S("n1_stat"), 1)
                    if n == F0 + 2:
                        pe.wait_ge(S("f_sin"), 1)
                        MM(bank[3][0:64, 0:SEQ], fw2[:, :], fh[:, 0, :], start=True, stop=True).then_inc(S("f_mm"), 1)
                    if n == F0 + 4:
                        pe.wait_ge(S("f_sin"), 2)
                        for t in range(2):
                            MM(bank[4 + t][:, :], fh[:, 1, t * P:(t + 1) * P], fw3[:, :], start=True, stop=True).then_inc(S("f_mm"), 1)
                    if n == F0 + 6:
                        pe.wait_ge(S("f_abs"), 2)
                        for t in range(2):
                            ins = MM(bank[6][:, :], ones[:, :], habs[:, t, :], start=(t == 0), stop=(t == 1))
                        ins.then_inc(S("f_mm"), 1)
                    if n == at["in", 3]:
                        pe.wait_ge(S("q_ok"), 4)
                        pe.wait_ge(S("mean_sq"), 3)
                        pe.wait_ge(S("f_sd"), 1)
                        for f in range(2):
                            o = bank[3][:, f * SEQ:(f + 1) * SEQ]
                            for t in range(2):
                                MM(o, fwd0[:, 0, t, f * P:(f + 1) * P], hs[:, t, :], start=(t == 0), stop=False)
                            MM(o, ones[0:1, :], hrow_d[:, :], start=False, stop=True)
                        for f in range(2):
                            o = bank[4][:, f * SEQ:(f + 1) * SEQ]
                            for t in range(2):
                                ins = MM(o, fwd0[:, 1, t, f * P:(f + 1) * P], hd[:, t, :], start=(t == 0), stop=(t == 1))
                        ins.then_inc(S("f_mm"), 1)
                    if n == Q_SLOT:
                        pe.wait_ge(S("q_sq"), 4)
                        for i in range(4):
                            for t in range(NT):
                                c = t * NH + 2 * i
                                ins = MM(bank[5][:, c:c + 2], zsq[:, i, t * P:(t + 1) * P], headsum[:, :], start=True, stop=True)
                        ins.then_inc(S("q_stat"), 1)
                        for i in range(4):
                            pe.wait_ge(S("q_g"), i + 1)
                            MM(bank[2 + i // 2][:, (i % 2) * SEQ:(i % 2 + 1) * SEQ], rot[:, :], q[:, i, 0:SEQ], start=True, stop=True).then_inc(S("q_rot"), 1)
                    if n == K_SLOT:
                        pe.wait_ge(S("k_sq"), 1)
                        MM(bank[4][:, :], headmean[:, :], ksq[:, :], start=True, stop=True).then_inc(S("k_stat"), 1)
                        pe.wait_ge(S("mean_sq"), 2)
                        mv = first_tile[at["in", 2]] + 1
                        pe.wait_ge(S(f"zf{mv % 2}"), mv // 2 + 1)
                        for t in range(4):
                            ins = T_(bank[5][:, t * P:(t + 1) * P], vT[:, t * P:(t + 1) * P])
                        ins.then_inc(S("vrows"), 1)
                    if n == KROT_SLOT:
                        pe.wait_ge(S("k_g"), 1)
                        pe.wait_ge(S("H_ok"), 1)
                        MM(bank[4][:, 0:SEQ], rot[:, :], kraw[:, 0:SEQ], start=True, stop=True).then_inc(S("k_rot"), 1)
                    if n == U_SLOT:
                        pe.wait_ge(S("v_ok"), 1)
                        pe.wait_ge(S("q_ok"), 4)
                        pe.wait_ge(S("u"), 2)
                        for b in range(2):
                            for s in range(NS):
                                for c in range(2):
                                    o = s * SEQ + c * P
                                    ins = T_(bank[5 + b][:, o:o + P], zhy[:, 2 + c, s * SEQ + b * P:s * SEQ + (b + 1) * P])
                            ins.then_inc(S("uT"), 1)
                    if n == at["in", 6]:
                        pe.wait_ge(S("tab_in"), 32)
                        pe.wait_ge(S("u_act"), 1)
                        pe.wait_ge(S("u_dve"), 1)
                        pe.wait_ge(S("k_ok"), 1)
                        for f in range(2):
                            for part in range(2):
                                for t in range(2):
                                    ins = MM(bank[2 + 2 * f + part][:, 0:T], fwd[:, part, t, f * P:(f + 1) * P], urow[:, t, 0:T], start=(t == 0), stop=(t == 1))
                                ins.then_inc(S("U"), 1)
                    if n == Y_SLOT:
                        pe.wait_ge(S("Y"), 2 * NS)
                        for c in range(2):
                            for s in range(NS):
                                for f in range(2):
                                    for part in range(2):
                                        ins = MM(bank[5 + c][:, s * SEQ:(s + 1) * SEQ], Y[:, part, f, s * SEQ + c * P:s * SEQ + (c + 1) * P],
                                                 inv[:, part, f, :], start=(f + part == 0), stop=(f + part == 2))
                            ins.then_inc(S("y_hy"), 1)

                    i = n - HEAD0
                    if 1 <= i <= NH:
                        pe.wait_ge(S("probs"), NT * i)
                        pe.wait_ge(S("oh_lo"), 2)
                        if i >= 2:
                            pe.wait_ge(S("pT_act"), NS * (i - 1))
                            pe.wait_ge(S("pT_dve"), i - 1)
                        for half in range(2):
                            for kt in range(2):
                                for c in range(2):
                                    ins = T_(bank[5 + half][:, kt * 256 + c * P:kt * 256 + (c + 1) * P], probs[:, c, (2 * half + kt) * P:(2 * half + kt + 1) * P])
                            ins.then_inc(S("pT"), 1)
                    if 0 <= i < NH:
                        if i == 0:
                            pe.wait_ge(S("k_ok"), 1)
                            pe.wait_ge(S("q_ok"), 4)
                        else:
                            pe.wait_ge(S("exp"), NT * i)
                        b0 = 64 * (i % 2)
                        kk = kd[b0:b0 + 64, i // 4, :]
                        for c in range(NT):
                            qq = q[b0:b0 + 64, i // 2, c * P:(c + 1) * P]
                            if c < 2:
                                ins = MM(bank[2 + c][:, :], qq, kk, start=True, stop=True)
                            else:
                                ins = MM(bank[4][:, (c - 2) * 256:(c - 1) * 256], qq, kk[:, SEQ:TOK], start=True, stop=True)
                        ins.then_inc(S("score"), 1)
                    if 1 <= i <= NH:
                        if NS == 2:
                            pe.wait_ge(S("pT_act"), NS * (i - 1) + 1)
                            for kt in range(2):
                                for c in range(2):
                                    ins = T_(bank[5][:, kt * 256 + c * P:kt * 256 + (c + 1) * P], probs[:, 2, c * 256 + kt * P:c * 256 + (kt + 1) * P])
                            ins.then_inc(S("pT"), 1)
                        h = i - 1
                        if h % 2 == 0:
                            if h == 0:
                                pe.wait_ge(S("mod_done"), 2)
                            else:
                                pe.wait_ge(S("oa_lo"), h // 2)
                        vv = lambda kt: vr[:, kt, 64 * (h // 4):64 * (h // 4) + 64]
                        o = bank[7][64 * (h % 2):64 * (h % 2) + 64, :]
                        pe.wait_ge(S("pT_act"), NS * (i - 1) + 1)
                        pe.wait_ge(S("pT_dve"), i)
                        for kt in range(4):
                            ins = MM(o[:, 0:SEQ], vv(kt), pT[:, kt // 2, (kt % 2) * 256:(kt % 2 + 1) * 256], start=(kt == 0), stop=(kt == 3))
                        if NS == 2:
                            pe.wait_ge(S("pT_act"), NS * i)
                            for kt in range(2):
                                ins = MM(o[:, SEQ:TOK], vv(2 + kt), pT[:, 2, kt * 256:(kt + 1) * 256], start=(kt == 0), stop=(kt == 1))
                        ins.then_inc(S("pv"), 1)
                    if n == at["gate", 8]:
                        pe.wait_ge(S("conv_ok"), 1)
                        for t in range(2):
                            ins = MM(bank[5][:, 0:T], ones[:, :], conv[:, t, 0:T], start=(t == 0), stop=(t == 1))
                        ins.then_inc(S("cf_mean"), 1)
                    if n == at["gate", 9]:
                        pe.wait_ge(S("cf_sq"), 2)
                        for t in range(2):
                            ins = MM(bank[6][:, 0:T], ones[:, :], csq[:, t, 0:T], start=(t == 0), stop=(t == 1))
                        ins.then_inc(S("cf_var"), 1)

                square_sums(KT - 2, KT)
                pe.sem_inc(S("e_used"), EP)
                pe.sem_inc(S("g_rows"), 2)
                pe.wait_ge(S("x_back2"), 32)
                for k in range(KT):
                    pe.wait_ge(S("h2"), NS * (k + 1))
                    ins = MM(bank[7][0:NE, 0:T], wr[:, k, :], h2T[:, k, 0:T], start=(k == 0), stop=(k == KT - 1))
                    if k < 4:
                        for t in range(NT):
                            row = T_(row_bank(t)[:, k * P:(k + 1) * P], h2T[:, k, t * P:(t + 1) * P])
                            if k == 3:
                                row.then_inc(S("rows"), 1)
                ins.then_inc(S("lg"), 1)
                for t in range(NT):
                    if NT + t >= 7:
                        pe.wait_ge(S("row_lo"), 1)
                    for k in range(4):
                        row = T_(row_bank(NT + t)[:, k * P:(k + 1) * P], h2T[:, 4 + k, t * P:(t + 1) * P])
                    row.then_inc(S("rows"), 1)
                    if t == 0:
                        pe.wait_ge(S("lgT"), 1)
                        for tt_ in range(NT):
                            ins = T_(bank[7][:, tt_ * NE:(tt_ + 1) * NE], lgT[:, tt_ * P:(tt_ + 1) * P], NE)
                        ins.then_inc(S("logits"), 1)
                pe.wait_ge(S("routed"), 1)
                MM(bank[7][:, 0:NT * NE], before[:, :], rt[:, 5, 0:NT * NE], start=True, stop=False)
                MM(bank[7][:, 0:NT * NE], ones[:, :], mask_sums[:, 0:NT * NE], start=False, stop=True)
                ins = MM(bank[7][:, 64:64 + NE], ones[:, :], mask_sums[:, NT * NE:(NT + 1) * NE], start=True, stop=True)
                ins.then_inc(S("places"), 1)
                pe.wait_ge(S("row_lo"), 2 * NT)

                pe.wait_ge(S("items_ok"), 1)
                last = pe.value_load(items_i[0:1, NI:NI + 1], min_val=NE - 1, max_val=NI - 1)

                def pick_rows(i, q0, q1):
                    for q_ in range(q0, q1):
                        c, t, part = q_ // (2 * NT), q_ // 2 % NT, q_ % 2
                        if q_ == 0:
                            pe.wait_ge(S("pick"), i + 1)
                        ins = MM(bank[2 + c][:, :], pick[:, t, :], (t_hi, t_lo)[part][:, t, c * 512:(c + 1) * 512],
                                 start=(t + part == 0), stop=(t == NT - 1 and part == 1))
                        if t == NT - 1 and part == 1:
                            ins.then_inc(S("g_rows"), 1)

                def pick_columns(i, c):
                    pe.wait_ge(S(("xr_a", "xr_d")[c]), i + 1)
                    for k in range(4):
                        ins = T_(bank[4 + c][:, k * P:(k + 1) * P], xpick[:, (4 * c + k) * P:(4 * c + k + 1) * P])
                    ins.then_inc(S("g_cols"), 1)

                GSTEPS = (0, 0, 0, 0, 2, 4, 6, 8, 12) if NT == 4 else (0, 0, 0, 0, 0, 0, 0, 1, 4)

                def item(i, more):
                    pe.wait_ge(S("xg_hi"), i * 2 + 2)
                    pe.wait_ge(S("xg_lo"), i * 2 + 2)
                    for j in range(8):
                        pe.wait_ge(S("e_lo"), i * EW + j + 1 + EW)
                        hi = half_unit(whi, j % EP).rearrange("p (k n) -> p k n", k=2)
                        lo = half_unit(wlo, j % EP).rearrange("p (k n) -> p k n", k=2)
                        for k in range(2):
                            kk = 2 * (j % 4) + k
                            o = bank[j // 4][:, :]
                            MM(o, xg_hi[:, kk, :], hi[:, k, :], start=(kk == 0), stop=False)
                            MM(o, xg_hi[:, kk, :], lo[:, k, :], start=False, stop=False)
                            ins = MM(o, xg_lo[:, kk, :], hi[:, k, :], start=False, stop=(kk == KT - 1))
                        ins.then_inc(S("e_used"), 1)
                        if more and j < 2:
                            pick_columns(i + 1, j)
                        if more and j == 3:
                            pe.wait_ge(S("xr_a"), i + 2)
                            pe.wait_ge(S("xr_d"), i + 2)
                        if more:
                            pick_rows(i + 2, GSTEPS[j], GSTEPS[j + 1])
                    pe.wait_ge(S("act_a"), i + 1)
                    for k in range(4):
                        ins = T_(bank[0][:, k * P:(k + 1) * P], act_a[:, k * P:(k + 1) * P])
                    ins.then_inc(S("aT"), 1)
                    if more:
                        pick_rows(i + 2, GSTEPS[8], 4 * NT)
                    pe.wait_ge(S("a_hi"), i + 1)
                    pe.wait_ge(S("a_lo"), i + 1)
                    pe.wait_ge(S("e_yev"), i + 1)
                    for j in range(8, EW):
                        pe.wait_ge(S("e_lo"), i * EW + j + 1 + EW)
                        hi, lo = half_unit(whi, j % EP), half_unit(wlo, j % EP)
                        kk = j - 8
                        for c in range(2):
                            o = bank[6 + c][:, :]
                            cc = slice(c * 512, (c + 1) * 512)
                            MM(o, a_hi[:, kk, :], hi[:, cc], start=(kk == 0), stop=False)
                            MM(o, a_hi[:, kk, :], lo[:, cc], start=False, stop=False)
                            ins = MM(o, a_lo[:, kk, :], hi[:, cc], start=False, stop=(kk == 3))
                        ins.then_inc(S("e_used"), 1)

                pick_rows(0, 0, 4 * NT)
                pick_columns(0, 0)
                pick_columns(0, 1)
                pick_rows(1, 0, 4 * NT)
                with pe.Fori(0, last) as i:
                    item(i, True)
                item(last, False)
                for t in range(NT):
                    pe.wait_ge(S("combined"), t + 1)
                    if t >= 2:
                        pe.wait_ge(S("x_moe"), (t - 1) * KT)
                    for k in range(KT):
                        b = 2 * (t % 2) + k // 4
                        ins = T_(bank[b][:, (k % 4) * P:(k % 4 + 1) * P], comb[:, t % 2, k * P:(k + 1) * P])
                    ins.then_inc(S("combT"), 1)
                pe.sem_inc(sem("all", "engine_done"), 1)
                if l == DEPTH - 1:
                    pe.wait_ge(S("moe_x"), 1)
                    for t in range(2):
                        for c in range(2):
                            for k in range(4):
                                ins = T_(bank[2 * t + c][:, k * P:(k + 1) * P], xT[:, 4 * c + k, t * P:(t + 1) * P])
                            ins.then_inc(sem("all", "oT"), 1)


_INS = ["x", "c", "ctx", "c_ctx", "w_mod", "b_mod", "g_norm1", "g_norm2", "w_in", "q_norm", "k_norm",
        "hy_short_w", "hy_short_b", "hy_w1", "hy_b1", "hy_w2", "hy_b2", "hy_w3", "hy_freq", "hy_bias",
        "cf_dw_w", "cf_dw_b", "cf_ln_g", "cf_ln_b", "p_attn", "p_hyena", "p_conv", "w_out",
        "w_router", "b_router", "w_exp_gate", "w_exp_up", "w_exp_down"]


def kernel(**inputs):
    import numpy as _np
    import concourse.bacc as _bacc
    from concourse import mybir as _mybir
    from concourse.bass_utils import run_bass_kernel_spmd as _run

    nc = _bacc.Bacc("TRN2", target_bir_lowering=False, num_devices=1)
    consts, f32 = shape_constants(inputs["x"].shape[1], inputs["x"].shape[2] // 4)
    arrays, aps = {}, {}
    for name in _INS:
        arrays[f"in_{name}"] = _np.ascontiguousarray(inputs[name])
    for name, a in consts.items():
        arrays[f"in_{name}"] = _np.ascontiguousarray(_np.asarray(a, dtype=f32))
    for name, a in arrays.items():
        aps[name[3:]] = nc.dram_tensor(name, a.shape, _mybir.dt.from_np(a.dtype), kind="ExternalInput").ap()
    out = nc.dram_tensor("out_0", inputs["x"].shape, _mybir.dt.float32, kind="ExternalOutput").ap()
    hybrid_backbone(nc, aps, out)
    r = _run(nc, [arrays], core_ids=[0])
    return r.results[0]["out_0"]
```
